# Optimizing a Trainium2 kernel written in Bass

```python
import math
import jax, jax.numpy as jnp
from jax import lax
import numpy as np

D_MODEL = 1024
BATCH = 1
SEQ = 1024
DEPTH = 2

N_MIXERS = 2
N_A_LAYERS = (DEPTH + 1) // 2
N_B_LAYERS = DEPTH // 2
EPS = 1e-6

A_HEADS = D_MODEL // 128
A_DK = 128
A_DV = 256
A_QK = A_HEADS * A_DK
A_VW = A_HEADS * A_DV
A_CONV = 4
A_CHUNK = 64
A_IN = 2 * A_QK + 2 * A_VW + 2 * A_HEADS

B_WINDOWS = (128, 512, 2048)
B_DILATIONS = (1, 4, 16)
B_GROUPS = len(B_WINDOWS)
B_HEADS = D_MODEL // 128
B_DH = 128
B_W = B_HEADS * B_DH
B_BLOCK = 128
B_IN = 3 * B_GROUPS * B_W + B_W
ROPE_THETA = 500000.0
ROPE_DIMS = B_DH // 4

kernel_name = "hybrid_gdn_dilated_swa"

def rms_norm(x, g):
    xf = x.astype(jnp.float32)
    y = xf * lax.rsqrt(jnp.mean(xf * xf, axis=-1, keepdims=True) + EPS)
    return (y * g.astype(jnp.float32)).astype(x.dtype)

def l2_norm(x):
    xf = x.astype(jnp.float32)
    return xf * lax.rsqrt(jnp.sum(xf * xf, axis=-1, keepdims=True) + EPS)

def causal_dwconv(x, w):
    K = w.shape[0]
    return lax.conv_general_dilated(
        x, w[:, None, :].astype(x.dtype), window_strides=(1,), padding=((K - 1, 0),),
        dimension_numbers=("NWC", "WIO", "NWC"), feature_group_count=x.shape[-1])

def gated_delta_rule(q, k, v, g, beta):
    Bn, H, S, DK = q.shape
    DV = v.shape[-1]
    C = A_CHUNK
    N = S // C
    f32 = jnp.float32
    q, k, v, g, beta = (t.astype(f32) for t in (q, k, v, g, beta))
    q = q * (DK ** -0.5)

    def chunk(t):
        return t.reshape((Bn, H, N, C) + t.shape[3:])

    q, k, v, g, beta = map(chunk, (q, k, v, g, beta))
    g = jnp.cumsum(g, axis=-1)
    idx = jnp.arange(C)
    causal = idx[:, None] >= idx[None, :]
    strict = idx[:, None] > idx[None, :]
    decay = jnp.exp(jnp.where(causal, g[..., :, None] - g[..., None, :], -jnp.inf))
    k_beta = k * beta[..., None]
    lower = jnp.where(strict, jnp.einsum("bhnid,bhnjd->bhnij", k_beta, k) * decay, 0.0)
    rhs = jnp.concatenate([v * beta[..., None], k_beta * jnp.exp(g)[..., None]], axis=-1)
    sol = lax.linalg.triangular_solve(lower + jnp.eye(C, dtype=f32), rhs,
                                      left_side=True, lower=True, unit_diagonal=True)
    u, w = sol[..., :DV], sol[..., DV:]
    qk = jnp.einsum("bhnid,bhnjd->bhnij", q, k) * decay

    def step(state, inp):
        q_c, k_c, u_c, w_c, g_c, qk_c = inp
        v_new = u_c - jnp.einsum("bhck,bhkv->bhcv", w_c, state)
        o = (jnp.einsum("bhck,bhkv->bhcv", q_c * jnp.exp(g_c)[..., None], state)
             + jnp.einsum("bhij,bhjv->bhiv", qk_c, v_new))
        g_last = g_c[..., -1:]
        state = (state * jnp.exp(g_last)[..., None]
                 + jnp.einsum("bhck,bhcv->bhkv", k_c * jnp.exp(g_last - g_c)[..., None], v_new))
        return state, o

    xs = tuple(jnp.moveaxis(t, 2, 0) for t in (q, k, u, w, g, qk))
    state0 = jnp.zeros((Bn, H, DK, DV), f32)
    _, o = lax.scan(step, state0, xs)
    return jnp.moveaxis(o, 0, 2).reshape(Bn, H, S, DV)

def gated_deltanet_mixer(h, w_in, conv_w, a_log, dt_bias, out_norm_g, w_out):
    Bn, S, _ = h.shape
    proj = h @ w_in
    n_qkv = 2 * A_QK + A_VW
    qkv = proj[..., :n_qkv]
    z = proj[..., n_qkv:n_qkv + A_VW]
    b_logit = proj[..., n_qkv + A_VW:n_qkv + A_VW + A_HEADS]
    a_logit = proj[..., n_qkv + A_VW + A_HEADS:]
    qkv = jax.nn.silu(causal_dwconv(qkv, conv_w))
    q = qkv[..., :A_QK].reshape(Bn, S, A_HEADS, A_DK).transpose(0, 2, 1, 3)
    k = qkv[..., A_QK:2 * A_QK].reshape(Bn, S, A_HEADS, A_DK).transpose(0, 2, 1, 3)
    v = qkv[..., 2 * A_QK:].reshape(Bn, S, A_HEADS, A_DV).transpose(0, 2, 1, 3)
    q, k = l2_norm(q), l2_norm(k)
    beta = jax.nn.sigmoid(b_logit.astype(jnp.float32)).transpose(0, 2, 1)
    g = (-jnp.exp(a_log.astype(jnp.float32))
         * jax.nn.softplus(a_logit.astype(jnp.float32) + dt_bias.astype(jnp.float32))).transpose(0, 2, 1)
    o = gated_delta_rule(q, k, v, g, beta).transpose(0, 2, 1, 3)
    o = rms_norm(o, out_norm_g).astype(h.dtype)
    o = o * jax.nn.silu(z.reshape(Bn, S, A_HEADS, A_DV))
    return o.reshape(Bn, S, A_VW) @ w_out

def partial_rope(x, cos, sin):
    half = ROPE_DIMS // 2
    x1, x2, xp = x[..., :half], x[..., half:ROPE_DIMS], x[..., ROPE_DIMS:]
    xf1, xf2 = x1.astype(jnp.float32), x2.astype(jnp.float32)
    r1 = (xf1 * cos - xf2 * sin).astype(x.dtype)
    r2 = (xf2 * cos + xf1 * sin).astype(x.dtype)
    return jnp.concatenate([r1, r2, xp], axis=-1)

def dilated_window_attention(q, k, v, dilation, span):
    Bn, S, H, DH = q.shape
    L = S // dilation
    nb = -(-L // B_BLOCK)
    Lp = nb * B_BLOCK

    def to_sub(t):
        t = t.reshape(Bn, L, dilation, H, DH).transpose(0, 2, 3, 1, 4)
        return jnp.pad(t, ((0, 0), (0, 0), (0, 0), (0, Lp - L), (0, 0)))

    qs, ks, vs = map(to_sub, (q, k, v))
    qb = qs.reshape(Bn, dilation, H, nb, B_BLOCK, DH)

    def band(t):
        tp = jnp.pad(t, ((0, 0), (0, 0), (0, 0), (B_BLOCK, 0), (0, 0)))
        prev = tp[..., :Lp, :].reshape(Bn, dilation, H, nb, B_BLOCK, DH)
        cur = tp[..., B_BLOCK:, :].reshape(Bn, dilation, H, nb, B_BLOCK, DH)
        return jnp.concatenate([prev, cur], axis=-2)

    kb, vb = band(ks), band(vs)
    qi = jnp.arange(B_BLOCK)[:, None]
    kj = jnp.arange(2 * B_BLOCK)[None, :]
    dist = qi + B_BLOCK - kj
    key_pos = jnp.arange(nb)[:, None, None] * B_BLOCK + kj[None] - B_BLOCK
    mask = (dist >= 0) & (dist <= span) & (key_pos >= 0)
    s = jnp.einsum("bdhnqe,bdhnke->bdhnqk", qb, kb,
                   preferred_element_type=jnp.float32) * (DH ** -0.5)
    s = jnp.where(mask, s, -jnp.inf)
    lse = jax.nn.logsumexp(s, axis=-1)
    p = jnp.exp(s - lse[..., None])
    o = jnp.einsum("bdhnqk,bdhnke->bdhnqe", p.astype(v.dtype), vb,
                   preferred_element_type=jnp.float32)

    def from_sub(t):
        t = t.reshape((Bn, dilation, H, Lp) + t.shape[5:])[:, :, :, :L]
        t = jnp.moveaxis(t, 3, 1)
        return t.reshape((Bn, S, H) + t.shape[4:])

    return from_sub(o), from_sub(lse)

def dilated_attention_mixer(h, positions, w_in, q_norm_g, k_norm_g, w_out):
    Bn, S, _ = h.shape
    proj = h @ w_in
    n_qkv = 3 * B_GROUPS * B_W
    qkv = proj[..., :n_qkv].reshape(Bn, S, 3, B_GROUPS, B_HEADS, B_DH)
    z = proj[..., n_qkv:]
    q, k, v = qkv[:, :, 0], qkv[:, :, 1], qkv[:, :, 2]
    q = rms_norm(q, q_norm_g[:, None, :])
    k = rms_norm(k, k_norm_g[:, None, :])
    inv_freq = ROPE_THETA ** (-jnp.arange(0, ROPE_DIMS, 2, dtype=jnp.float32) / ROPE_DIMS)
    ang = positions.astype(jnp.float32)[..., None] * inv_freq
    cos = jnp.cos(ang)[:, :, None, None, :]
    sin = jnp.sin(ang)[:, :, None, None, :]
    q, k = partial_rope(q, cos, sin), partial_rope(k, cos, sin)
    outs, lses = [], []
    for gi in range(B_GROUPS):
        o_g, lse_g = dilated_window_attention(q[:, :, gi], k[:, :, gi], v[:, :, gi],
                                              B_DILATIONS[gi], B_WINDOWS[gi] // B_DILATIONS[gi])
        outs.append(o_g)
        lses.append(lse_g)
    wts = jax.nn.softmax(jnp.stack(lses, axis=0), axis=0)
    o = jnp.sum(wts[..., None] * jnp.stack(outs, axis=0), axis=0).astype(h.dtype)
    o = o.reshape(Bn, S, B_W) * jax.nn.silu(z)
    return o @ w_out

def setup_inputs(seed: int = 0) -> dict:
    key = jax.random.key(seed)
    ks = jax.random.split(key, 16)
    f32 = jnp.float32
    x = jax.random.normal(ks[0], (BATCH, SEQ, D_MODEL), f32)
    positions = jnp.broadcast_to(jnp.arange(SEQ, dtype=jnp.int32)[None, :], (BATCH, SEQ))
    norm_g = 1.0 + 0.02 * jax.random.normal(ks[1], (DEPTH, D_MODEL), f32)
    a_w_in = jax.random.normal(ks[2], (N_A_LAYERS, D_MODEL, A_IN), f32) * D_MODEL ** -0.5
    a_conv_w = jax.random.normal(ks[3], (N_A_LAYERS, A_CONV, 2 * A_QK + A_VW), f32) * A_CONV ** -0.5
    a_log = jnp.log(jax.random.uniform(ks[4], (N_A_LAYERS, A_HEADS), f32, 1.0, 16.0))
    dt = jnp.exp(jax.random.uniform(ks[5], (N_A_LAYERS, A_HEADS), f32,
                                    math.log(1e-3), math.log(1e-1)))
    a_dt_bias = dt + jnp.log(-jnp.expm1(-dt))
    a_norm_g = 1.0 + 0.02 * jax.random.normal(ks[6], (N_A_LAYERS, A_DV), f32)
    a_w_out = jax.random.normal(ks[7], (N_A_LAYERS, A_VW, D_MODEL), f32) * A_VW ** -0.5
    b_w_in = jax.random.normal(ks[8], (N_B_LAYERS, D_MODEL, B_IN), f32) * D_MODEL ** -0.5
    b_q_norm_g = 1.0 + 0.02 * jax.random.normal(ks[9], (N_B_LAYERS, B_GROUPS, B_DH), f32)
    b_k_norm_g = 1.0 + 0.02 * jax.random.normal(ks[10], (N_B_LAYERS, B_GROUPS, B_DH), f32)
    b_w_out = jax.random.normal(ks[11], (N_B_LAYERS, B_W, D_MODEL), f32) * B_W ** -0.5
    return {"x": x, "positions": positions, "norm_g": norm_g,
            "a_w_in": a_w_in, "a_conv_w": a_conv_w, "a_log": a_log, "a_dt_bias": a_dt_bias,
            "a_norm_g": a_norm_g, "a_w_out": a_w_out,
            "b_w_in": b_w_in, "b_q_norm_g": b_q_norm_g, "b_k_norm_g": b_k_norm_g,
            "b_w_out": b_w_out}

def reference(x, positions, norm_g, a_w_in, a_conv_w, a_log, a_dt_bias, a_norm_g, a_w_out,
              b_w_in, b_q_norm_g, b_k_norm_g, b_w_out):
    for i in range(DEPTH):
        h = rms_norm(x, norm_g[i])
        j = i // N_MIXERS
        if i % N_MIXERS == 0:
            y = gated_deltanet_mixer(h, a_w_in[j], a_conv_w[j], a_log[j], a_dt_bias[j],
                                     a_norm_g[j], a_w_out[j])
        else:
            y = dilated_attention_mixer(h, positions, b_w_in[j], b_q_norm_g[j],
                                        b_k_norm_g[j], b_w_out[j])
        x = x + y.astype(x.dtype)
    return x


_drawn_inputs = setup_inputs


def setup_inputs(seed=0):
    import zlib

    import numpy as np

    out = dict(_drawn_inputs(seed))
    spreads = {}
    factors = {'norm_g': 3.241, 'a_norm_g': 5.411, 'b_q_norm_g': 8.0, 'b_k_norm_g': 8.0}
    for name, (base, spread) in spreads.items():
        noise = np.random.default_rng([zlib.crc32(name.encode()), seed]).standard_normal(out[name].shape)
        drawn = base * np.exp(spread * noise) if base else spread * noise
        out[name] = __import__('jax').numpy.asarray(drawn.astype(out[name].dtype))
    for name, factor in factors.items():
        out[name] = (out[name] * factor).astype(out[name].dtype)
    return out
```

```python
from contextlib import ExitStack

import numpy as np

import concourse.bass as bass
from concourse import mybir

F32 = mybir.dt.float32
F32R = mybir.dt.float32r
I32 = mybir.dt.int32
ALU = mybir.AluOpType
ACT = mybir.ActivationFunctionType
AX = mybir.AxisListType

P = 128
S = 1024
D = 1024
T = S // P
KD = D // P
HALF = 512
TH = HALF // P
H = D // P
DK = 128
DV = 256
VT = DV // P
A_QK = H * DK
A_VW = H * DV
CONV = 4
CT = (2 * A_QK + A_VW) // P
EPS = 1e-6
EXP_LN = "natural_log_exp_and_others"
BIG = 1e30
ARG_MAX = 44.0
BLK = 16
NB = P // BLK
LEVELS = 3
BLOCK_STEP = BLK * (P + 1)
TILE_STEP = NB * BLOCK_STEP

DIL = (1, 4, 16)
NG = len(DIL)
ROPE = 32
HR = ROPE // 2
THETA = 500000.0


def spread(ap, axis, n):
    v = ap.unsqueeze(axis)
    shape = list(v.shape)
    shape[axis] = n
    return v.broadcast_to(shape)


class Mem:

    def __init__(self, nc, ctx, tag):
        self.nc, self.ctx, self.tag = nc, ctx, tag

    def sb(self, name, shape, dt=F32):
        return self.ctx.enter_context(self.nc.sbuf_tensor(f"{self.tag}_{name}", shape, dt))

    def ps(self, name, shape, dt=F32):
        return self.ctx.enter_context(self.nc.psum_tensor(f"{self.tag}_{name}", shape, dt))

    def sem(self, name):
        return self.ctx.enter_context(self.nc.semaphore(f"{self.tag}_{name}"))


def constants(nc, g, norm_g, a_norm_g, b_q_norm_g, b_k_norm_g, a_conv_w, a_log, a_dt_bias):
    with ExitStack() as ctx:
        m = Mem(nc, ctx, "c")
        rows = m.sb("rows", [24, P])
        conv_rows = m.sb("conv_rows", [P, P])
        head_row = m.sb("head_row", [1, 2 * H])
        ps = m.ps("ps", [P, 512])
        zero = m.sem("zero")
        made = m.sem("made")
        landed = m.sem("landed")
        turned = m.sem("turned")
        kept = m.sem("kept")
        block = ctx.enter_context(nc.Block())

        @block.sync
        def _(sp):
            sp.dma_start(rows[0:16, :], norm_g.rearrange("l (k c) -> (l k) c", c=P)).then_inc(landed, 16)
            sp.dma_start(rows[16:18, :], a_norm_g.rearrange("l (k c) -> (l k) c", c=P)).then_inc(landed, 16)
            sp.dma_start(rows[18:21, :], b_q_norm_g.rearrange("l g c -> (l g) c")).then_inc(landed, 16)
            sp.dma_start(rows[21:24, :], b_k_norm_g.rearrange("l g c -> (l g) c")).then_inc(landed, 16)
            sp.dma_start(conv_rows[:, :], a_conv_w.rearrange("l j (c n) -> (l j c) n", n=P)).then_inc(landed, 16)
            sp.dma_start(head_row[:, 0:H], a_log).then_inc(landed, 16)
            sp.dma_start(head_row[:, H:2 * H], a_dt_bias).then_inc(landed, 16)

        @block.gpsimd
        def _(pool):
            def ones(ap):
                pool.memset(ap, 1.0).then_inc(zero, 1)

            cuts = []

            def keep(ap, pattern, base, mult, op, fill):
                if cuts:
                    pool.wait_ge(made, len(cuts))
                cuts.append(ap)
                pool.affine_select(out=ap, in_=ap, compare_op=op, fill=fill, base=base,
                                   pattern=pattern, channel_multiplier=mult).then_inc(made, 1)

            ones(g.ones[:, :])
            pool.memset(g.ident[:, :], 0.0).then_inc(zero, 1)
            ones(g.tri[:, :])
            pool.memset(g.decay_mask[:, :], 0.0).then_inc(zero, 1)
            ones(g.level_mask[:, :, :])
            pool.wait_ge(zero, 5)
            keep(g.ident[:, :], [[-1, P]], 0, 1, ALU.not_equal, 1.0)
            keep(g.tri[:, :], [[1, P]], 0, -1, ALU.is_ge, 0.0)
            keep(g.decay_mask[:, :], [[1, P]], 0, -1, ALU.is_ge, -BIG)
            for level in range(LEVELS):
                size = BLK << level
                pairs = P // (2 * size)
                cell = g.level_mask[:, level, :].rearrange("p (c e r) -> p c e r", e=2, r=size)
                for across, within, base, mult in ((0, 1, -1, 0), (-2 * size, 0, 0, 1), (2 * size, 0, size - 1, -1)):
                    if pairs > 1:
                        keep(cell, [[across, pairs], [within, 2], [0, size]], base, mult, ALU.is_ge, 0.0)
                    else:
                        keep(cell[:, 0], [[within, 2], [0, size]], base, mult, ALU.is_ge, 0.0)
            pool.wait_ge(made, len(cuts))

        @block.tensor
        def _(pe):
            pe.wait_ge(landed, 7 * 16)
            pe.wait_ge(made, 1)
            pe.transpose(ps[:, 0:24], rows[:, :], g.ident[0:24, 0:24])
            pe.transpose(ps[:, 128:256], conv_rows[:, :], g.ident[:, :])
            pe.matmul(ps[:, 256:256 + 2 * H], g.ones[0:1, :], head_row[:, :], start=True, stop=True).then_inc(turned, 1)

        @block.vector
        def _(dve):
            dve.wait_ge(turned, 1)
            dve.tensor_copy(g.gains[:, :], ps[:, 0:24]).then_inc(kept, 1)
            dve.tensor_copy(g.conv[:, :, :], ps[:, 128:256].rearrange("p (j c) -> p j c", j=CONV)).then_inc(kept, 1)
            dve.tensor_copy(g.head_bc[:, :], ps[:, 256:256 + 2 * H]).then_inc(kept, 1)


def norm_and_turn(nc, tag, g, src, layer):
    with ExitStack() as ctx:
        m = Mem(nc, ctx, tag)
        x = m.sb("x", [P, 2, D])
        xn = m.sb("xn", [P, 2, D])
        sq = m.sb("sq", [P, D])
        stat = m.sb("stat", [P, 2, 4])
        hf = m.sb("hf", [P, 2, KD, P])
        turned_ps = m.ps("turned_ps", [P, 2, KD, P])
        landed = [m.sem("landed0"), m.sem("landed1")]
        stats = m.sem("stats")
        scaled = m.sem("scaled")
        turned = m.sem("turned")
        gained = m.sem("gained")
        high = m.sem("high")
        low = m.sem("low")
        block = ctx.enter_context(nc.Block())
        gain = g.gains[:, layer * KD:(layer + 1) * KD]

        def pairs(eng, body):
            body(0, True)
            with eng.Fori(1, T // 2) as i:
                body(i, False)

        @block.sync
        def _(sp):
            def load(i, first):
                for b in range(2):
                    if not first:
                        sp.wait_ge(scaled, 2 * i + b - 1)
                    sp.dma_start(x[:, b, :], src[bass.ds(i * (2 * P) + b * P, P), :]).then_inc(landed[b], 16)
            pairs(sp, load)

        @block.scalar
        def _(act):
            def scale(i, first):
                for b in range(2):
                    act.wait_ge(landed[b], 16 * i + 16)
                    act.activation(sq[:, :], x[:, b, :], ACT.Square, accum_out=stat[:, b, 0:1]).then_inc(stats, 1)
                    act.wait_ge(stats, 6 * i + 3 * b + 1)
                    act.activation(stat[:, b, 1:2], stat[:, b, 0:1], ACT.Ln, scale=1.0 / D, bias=EPS).then_inc(stats, 1)
                    act.wait_ge(stats, 6 * i + 3 * b + 2)
                    act.activation(stat[:, b, 2:3], stat[:, b, 1:2], ACT.Exp, scale=-0.5).then_inc(stats, 1)
                    act.wait_ge(stats, 6 * i + 3 * b + 3)
                    if not first:
                        act.wait_ge(turned, 2 * i + b - 1)
                    act.activation(xn[:, b, :], x[:, b, :], ACT.Copy, scale=stat[:, b, 2:3]).then_inc(scaled, 1)
                for b in range(2):
                    act.wait_ge(gained, 2 * i + b + 1)
                    act.activation(g.h_hi[:, :, bass.ds(i * (2 * P) + b * P, P)], hf[:, b], ACT.Copy).then_inc(high, 1)
            pairs(act, scale)

        @block.tensor
        def _(pe):
            def turn(i, first):
                for b in range(2):
                    pe.wait_ge(scaled, 2 * i + b + 1)
                    if not first:
                        pe.wait_ge(gained, 2 * i + b - 1)
                    for k in range(KD):
                        last = pe.transpose(turned_ps[:, b, k, :], xn[:, b, k * P:(k + 1) * P], g.ident[:, :])
                    last.then_inc(turned, 1)
            pairs(pe, turn)

        @block.vector
        def _(dve):
            def gain_and_split(i, first):
                for b in range(2):
                    dve.wait_ge(turned, 2 * i + b + 1)
                    if not first:
                        dve.wait_ge(high, 2 * i + b - 1)
                    dve.tensor_tensor(hf[:, b], turned_ps[:, b], spread(gain, 2, P),
                                      ALU.mult).then_inc(gained, 1)
                    dve.wait_ge(gained, 2 * i + b + 1)
                    dve.wait_ge(high, 2 * i + b + 1)
                    col = bass.ds(i * (2 * P) + b * P, P)
                    dve.tensor_tensor(g.h_lo[:, :, col], hf[:, b], g.h_hi[:, :, col].bitcast(F32),
                                      ALU.subtract).then_inc(low, 1)
            pairs(dve, gain_and_split)


SLOTS = 36
UNITS = 6
HALVES = 2 * UNITS
LEVEL0 = 2
DECAYS = (12, 15)
CHAIN0 = 8
K_TURNS = (22, 34)
GRAM0 = 18
BLOCKS_OUT = GRAM0 + T + 1
DELAYED = SLOTS + 6


def three_passes(pe, out, w_hi, w_lo, a_hi, a_lo, ks, third):
    last = None
    for n in range(8 * third, 8 * third + 8):
        k, c = n // 3, n % 3
        w = (w_hi, w_hi, w_lo)[c]
        a = (a_hi, a_lo, a_hi)[c]
        last = pe.matmul(out, w[:, k, :], a[:, k, ks], start=(n == 0), stop=(n == 23))
    return last


def delta_heads(nc, g, a_w_in, o_turned):
    with ExitStack() as ctx:
        m_ = Mem(nc, ctx, "a")
        raw = m_.sb("raw", [P, 2, KD, P])
        w_hi = [m_.sb(f"w_hi{i}", [P, KD, P], F32R) for i in range(2)]
        w_lo = [m_.sb(f"w_lo{i}", [P, KD, P], F32R) for i in range(2)]
        x_raw = m_.sb("x_raw", [P, CONV - 1 + S])
        acc = m_.sb("acc", [P, 2, HALF])
        sg = m_.sb("sg", [P, 2, HALF])
        kq = m_.sb("kq", [P, 2, T, 2, P])
        v = m_.sb("v", [P, 2, T, DV])
        z = m_.sb("z", [P, 2, VT, S])
        attn = m_.sb("attn", [P, 2, T, P])
        kd = m_.sb("kd", [P, T, P])
        u = m_.sb("u", [P, T, P])
        zx = m_.sb("zx", [P, T, 2, P])
        zf = m_.sb("zf", [P, T, P])
        cols = m_.sb("cols", [P, 7, T, H])
        hc = m_.sb("hc", [P, 2, 7, T])
        hw = m_.sb("hw", [P, 2, CONV, 4])
        bd = m_.sb("bd", [NB * T, BLK, BLK])
        bx = m_.sb("bx", [NB * T, BLK, BLK])
        bt = m_.sb("bt", [NB * T, (BLK // 2) ** 2])
        dec = m_.sb("dec", [P, T, P])
        um = m_.sb("um", [P, 2, LEVELS, P])
        bc = m_.sb("bc", [P, 2, P])
        zx1 = m_.sb("zx1", [P, 2, 2, P])
        state = m_.sb("state", [P, 2, DV])
        r = m_.sb("r", [P, DV])
        vn = m_.sb("vn", [P, DV])
        o1 = m_.sb("o1", [P, 2, DV])
        o = m_.sb("o", [P, 2, DV])
        ostat = m_.sb("ostat", [P, 2, 3])
        og = m_.sb("og", [P, VT, P])
        ba = acc[0:2 * H].rearrange("p b i -> p (b i)")
        tmp = sg[:, 0, 0:3 * T * H].rearrange("p (a t h) -> p a t h", a=3, t=T)
        neg_a = m_.sb("neg_a", [P, H])
        C_CUM, C_EXP, C_NEXP, C_BETA, C_TAIL, C_LAST, C_LOG = range(7)

        u_dram = nc.dram_tensor("u_tiles", [T * TILE_STEP], F32, kind="Internal").ap()
        inv_dram = nc.dram_tensor("inverse_tiles", [2, T * TILE_STEP], F32, kind="Internal").ap()

        def as_tiles(flat):
            return (flat.rearrange("(t x) -> t x", x=TILE_STEP)[:, 0:P * P]
                    .rearrange("t (j i) -> j t i", j=P))

        def as_blocks(flat):
            return (flat.rearrange("(p x) -> p x", x=BLOCK_STEP)[:, 0:BLK * P]
                    .rearrange("p (j i) -> p j i", i=P)[:, :, 0:BLK])

        proj = [m_.ps(f"proj{i}", [P, HALF]) for i in range(2)]
        step = m_.ps("step", [P, 2, DV])
        new = m_.ps("new", [P, DV])
        first = m_.ps("first", [P, 2, P])
        lev = m_.ps("lev", [P, 2, 2, P])
        turn = m_.ps("turn", [P, HALF])
        gram = m_.ps("gram", [P, HALF])

        sem = m_.sem
        w_landed = [sem("w_landed0"), sem("w_landed1")]
        w_high, w_low = sem("w_high"), sem("w_low")
        proj_mm, evac = sem("proj_mm"), sem("evac")
        arg, sig, act_out = sem("arg"), sem("sig"), sem("act_out")
        sigs = sem("sigs")
        convs, taps = sem("convs"), sem("taps")
        sq, nsum, rs, rss, kqn = sem("sq"), sem("nsum"), sem("rs"), sem("rss"), sem("kqn")
        v_turned, v_kept = sem("v_turned"), sem("v_kept")
        k_turned, k_kept = sem("k_turned"), sem("k_kept")
        k_tail = sem("k_tail")
        row_mm = sem("row_mm")
        gram_mm, darg, dexp, ut = sem("gram_mm"), sem("darg"), sem("dexp"), sem("ut")
        blocks_out, blocks_in, blocks_inv = sem("blocks_out"), sem("blocks_in"), sem("blocks_inv")
        inv_out, inv_zero = sem("inv_out"), sem("inv_zero")
        back = [sem("back_first"), sem("back_rest")]
        bstep = sem("bstep")
        zx_zero = sem("zx_zero")
        um_s, first_mm, first_c, lv_mm, lv_s = (sem(x) for x in ("um", "first_mm", "first_c", "lv_mm", "lv_s"))
        ks_mm, r_s, xr_mm, vn_s = sem("ks_mm"), sem("r_s"), sem("xr_mm"), sem("vn_s")
        osu_mm, o1_s, st_s, o_s = sem("osu_mm"), sem("o1_s"), sem("st_s"), sem("o_s")
        ostats, on_s, o_mm, og_s = sem("ostats"), sem("on_s"), sem("o_mm"), sem("og_s")
        o_stored = sem("o_stored")
        hc_s = sem("hc_s")
        setup = sem("setup")
        cols_s = sem("cols_s")
        totals = sem("totals")
        carrier = sem("carrier")
        block = ctx.enter_context(nc.Block())

        def col_of(n, j):
            if j == 0:
                return n * P + A_QK
            if j == 1:
                return n * P
            if j < 4:
                return n * DV + (2 * A_QK + (j - 2) * P)
            return n * DV + (2 * A_QK + A_VW + (j - 4) * P)

        def slot_of(j):
            return (1 + j) % 2

        def landed_of(n, j):
            return 16 * (n * (UNITS // 2) + (1 + j) // 2 + 1)

        def turn_order(mix, nxt):
            uses = []
            for s in range(SLOTS):
                if mix and (s - CHAIN0 - 6) % 3 == 0 and 0 <= (s - CHAIN0 - 6) // 3 < T:
                    uses.append(("o", (s - CHAIN0 - 6) // 3))
                if nxt and s in (8, 11, 14, 17):
                    uses.append(("sum", (s - 8) // 3))
                if nxt and s in K_TURNS:
                    uses.append(("k", K_TURNS.index(s)))
                if nxt and s in (20, 23, 26, 29):
                    uses.append(("v", (s - 20) // 3))
            return uses

        def heads(eng, body):
            body(None, 0, 0)
            with eng.Fori(0, H // 2 - 1) as i:
                body(i * 2, i * 2 + 1, 1)
                body(i * 2 + 1, i * 2 + 2, 0)
            body(H - 2, H - 1, 1)
            body(H - 1, None, 0)

        @block.sync
        def _(sp):
            base = 2 * A_QK + 2 * A_VW
            sp.wait_ge(setup, 1)
            sp.dma_start(raw[:, 0, :, 0:2 * H],
                         a_w_in[:, base:base + 2 * H].rearrange("(k p) c -> p k c", p=P)).then_inc(w_landed[0], 16)
            sp.dma_start(raw[:, 1], a_w_in[:, col_of(0, 0):col_of(0, 0) + P]
                         .rearrange("(k p) c -> p k c", p=P)).then_inc(w_landed[1], 16)

            def load(n, j):
                sp.wait_ge(w_low, n * UNITS + j)
                sp.sem_inc(carrier, 1)
                sp.dma_start(raw[:, slot_of(j)], a_w_in[:, bass.ds(col_of(n, j), P)]
                             .rearrange("(k p) c -> p k c", p=P)).then_inc(w_landed[slot_of(j)], 16)

            sp.wait_ge(zx_zero, 1)
            for c in range(2):
                sp.dma_start(as_tiles(inv_dram[c]), zx[:, :, c, :]).then_inc(inv_zero, 16)
            sp.wait_ge(inv_zero, 32)

            def body(m, n, p):
                for s in range(DELAYED):
                    if m is not None and s == 0:
                        sp.wait_ge(blocks_inv, m * 2 + 2)
                        sp.wait_ge(lv_s, m * (LEVELS * T // 2) + 1)
                        sp.dma_start(as_blocks(inv_dram[0]), bd[:, :, :]).then_inc(inv_out, 16)
                        sp.dma_start(as_blocks(inv_dram[1]), bx[:, :, :]).then_inc(inv_out, 16)
                        sp.wait_ge(inv_out, m * 32 + 32)
                        for part, tiles in enumerate((slice(0, 2), slice(2, T))):
                            for c in range(2):
                                sp.dma_start(zx[:, tiles, c, :], as_tiles(inv_dram[c])[:, tiles]
                                             ).then_inc(back[part], 16)
                    if n is not None and s < SLOTS and s % 6 == 3:
                        j = s // 6 + 1
                        if j < UNITS:
                            load(n, j)
                        elif not (isinstance(n, int) and n == H - 1):
                            load(n + 1, 0)
                    if n is not None and s == BLOCKS_OUT:
                        sp.wait_ge(ut, n * (T // 2) + T // 2)
                        sp.dma_start(as_tiles(u_dram), u[:, :, :]).then_inc(blocks_out, 16)
                        if not (isinstance(n, int) and n == 0):
                            sp.wait_ge(inv_out, n * 32)
                        sp.wait_ge(blocks_out, n * 16 + 16)
                        sp.dma_start(bd[:, :, :], as_blocks(u_dram)).then_inc(blocks_in, 16)
                    if m is not None and (s - CHAIN0 - 8) % 3 == 0 and 0 <= (s - CHAIN0 - 8) // 3 < T:
                        t = (s - CHAIN0 - 8) // 3
                        sp.wait_ge(og_s, m * T + (t + 1 + T))
                        dst = o_turned[bass.ds(m * DV, DV), t * P:(t + 1) * P].rearrange("(c p) n -> p c n", p=P)
                        sp.dma_start(dst, og[:, :, :]).then_inc(o_stored, 16)

            heads(sp, body)
            sp.wait_ge(o_stored, 16 * (1 + H * T))

        @block.gpsimd
        def _(pool):
            pool.memset(zx[:, :, :, :], 0.0).then_inc(zx_zero, 1)
            pool.wait_ge(cols_s, 1)

            def body(m, n, p):
                if n is not None:
                    columns_and_taps(n, p)
                if m is not None:
                    for b in range(T // 2):
                        pool.wait_ge(first_mm, m * (LEVELS * T // 2) + (LEVELS * b + 1))
                        pool.wait_ge(ut, m * (T // 2) + (b + 1))
                        pool.tensor_tensor(um[:, :, :, :], spread(u[:, 2 * b:2 * b + 2, :], 2, LEVELS),
                                           spread(g.level_mask[:, :, :], 1, 2), ALU.mult).then_inc(um_s, 1)
                if n is not None:
                    invert_blocks(n)

            def columns_and_taps(n, p):
                pool.wait_ge(og_s, n * T)
                pool.tensor_copy(hc[:, p], cols[:, :, :, bass.ds(n, 1)].rearrange("p a t o -> p a (t o)")
                                 ).then_inc(hc_s, 1)
                for c, tile in ((0, n + H), (1, n + 0), (2, n * 2 + 2 * H), (3, n * 2 + (2 * H + 1))):
                    pool.tensor_copy(hw[:, p, :, c:c + 1], g.conv[:, :, bass.ds(tile, 1)]).then_inc(hc_s, 1)

            def invert_blocks(n):
                if not (isinstance(n, int) and n == 0):
                    pool.wait_ge(inv_out, n * 32)
                pool.sem_inc(carrier, 1)
                pool.memset(bx[:, :, :], 0.0).then_inc(bstep, 1)
                pool.wait_ge(bstep, n * (2 * BLK) + 1)
                pool.sem_inc(carrier, 1)
                pool.tensor_copy(bx[:, :, :].rearrange("t j i -> t (j i)")[:, 0:BLK * BLK:BLK + 1],
                                 g.ones[0:NB * T, 0:BLK]).then_inc(bstep, 1)
                pool.wait_ge(blocks_in, n * 16 + 16)
                for j in range(BLK - 1):
                    pool.wait_ge(bstep, n * (2 * BLK) + (2 + 2 * j))
                    rows, width = BLK - 1 - j, j + 1
                    prod = bt[:, 0:rows * width].rearrange("t (i c) -> t i c", c=width)
                    pool.tensor_tensor(prod, spread(bd[:, j, j + 1:BLK], 2, width),
                                       spread(bx[:, j, 0:width], 1, rows), ALU.mult).then_inc(bstep, 1)
                    pool.wait_ge(bstep, n * (2 * BLK) + (3 + 2 * j))
                    pool.tensor_tensor(bx[:, j + 1:BLK, 0:width], bx[:, j + 1:BLK, 0:width], prod,
                                       ALU.subtract).then_inc(bstep if j < BLK - 2 else blocks_inv, 1)
                pool.wait_ge(blocks_inv, n * 2 + 1)
                pool.sem_inc(carrier, 1)
                pool.tensor_copy(bd[:, :, :], bx[:, :, :].rearrange("t i c -> t c i")).then_inc(blocks_inv, 1)
                pool.wait_ge(blocks_inv, n * 2 + 2)
                pool.sem_inc(bstep, 1)

            heads(pool, body)

        @block.scalar
        def _(act):
            def split_high(idx, slot, landed, first=False):
                act.wait_ge(w_landed[slot], landed)
                if not first:
                    act.wait_ge(proj_mm, idx * 2 - 2)
                act.activation(w_hi[slot][:, :, :], raw[:, slot], ACT.Copy).then_inc(w_high, 1)

            act.preload_act_table_set(EXP_LN)
            split_high(0, 0, 16, True)
            split_high(1, 1, 16, True)
            for b in range(2):
                act.wait_ge(proj_mm, b + 1)
                act.activation(ba[:, b * HALF:(b + 1) * HALF], proj[b][0:2 * H, :], ACT.Copy).then_inc(evac, 1)
            act.wait_ge(setup, 3)
            act.activation(neg_a[:, :], g.head_bc[:, 0:H], ACT.Exp).then_inc(setup, 1)
            act.activation(tmp[:, 0], tmp[:, 0], ACT.Exp).then_inc(setup, 1)
            act.activation(tmp[:, 2], tmp[:, 1], ACT.Abs).then_inc(setup, 1)
            act.wait_ge(setup, 6)
            act.activation(tmp[:, 0], tmp[:, 0], ACT.Ln, bias=1.0).then_inc(setup, 1)
            act.activation(tmp[:, 2], tmp[:, 2], ACT.Exp, scale=-1.0).then_inc(setup, 1)
            act.wait_ge(setup, 8)
            act.activation(cols[:, C_BETA], tmp[:, 0], ACT.Exp, scale=-1.0).then_inc(setup, 1)
            act.activation(tmp[:, 2], tmp[:, 2], ACT.Ln, bias=1.0).then_inc(setup, 1)
            act.wait_ge(setup, 14)
            act.activation(cols[:, C_EXP], cols[:, C_CUM], ACT.Exp).then_inc(setup, 1)
            act.activation(cols[:, C_LAST], tmp[:, 0], ACT.Exp).then_inc(setup, 1)
            act.activation(cols[:, C_TAIL], tmp[:, 1], ACT.Exp).then_inc(setup, 1)

            def body(m, n, p):
                pm = 1 - p
                for s in range(DELAYED):
                    if m is not None:
                        b, k = divmod(s - LEVEL0 - 1, 6)
                        if 0 <= b < T // 2 and k % 2 == 0:
                            use = LEVELS * b + k // 2
                            act.wait_ge(first_mm, m * (LEVELS * T // 2) + (use + 1 + 1))
                            act.activation(bc[:, :, :], first[:, :, :], ACT.Copy).then_inc(first_c, 1)
                        t, k = divmod(s - CHAIN0, 3)
                        if 0 <= t < T and k == 0:
                            act.wait_ge(r_s, m * T + (t + 1))
                            act.wait_ge(o_s, m * T + (t - 1 + 2))
                            act.wait_ge(ostats, m * (3 * T) + (3 * (t - 2) + 1 + 6))
                            act.activation(o1[:, t % 2, :], step[:, 1], ACT.Copy,
                                           scale=hc[:, pm, C_EXP, t:t + 1]).then_inc(o1_s, 1)
                        if 0 <= t < T and k == 1:
                            act.wait_ge(xr_mm, m * T + (t + 1))
                            act.wait_ge(osu_mm, m * T + (t + 1))
                            act.activation(vn[:, :], new[:, :], ACT.Copy,
                                           scale=hc[:, pm, C_BETA, t:t + 1]).then_inc(vn_s, 1)
                        t, k = divmod(s - CHAIN0 - 4, 3)
                        if 0 <= t < T and k == 0:
                            act.wait_ge(o_s, m * T + (t + 1 + 2))
                            act.activation(o1[:, t % 2, :], o[:, t % 2, :], ACT.Square,
                                           accum_out=ostat[:, t % 2, 0:1]).then_inc(ostats, 1)
                            act.wait_ge(ostats, m * (3 * T) + (3 * t + 1 + 6))
                            act.activation(ostat[:, t % 2, 1:2], ostat[:, t % 2, 0:1], ACT.Ln,
                                           scale=1.0 / DV, bias=EPS).then_inc(ostats, 1)
                            act.wait_ge(ostats, m * (3 * T) + (3 * t + 2 + 6))
                            act.activation(ostat[:, t % 2, 2:3], ostat[:, t % 2, 1:2], ACT.Exp,
                                           scale=-0.5).then_inc(ostats, 1)
                            act.wait_ge(ostats, m * (3 * T) + (3 * t + 3 + 6))
                            act.activation(o[:, t % 2, :], o[:, t % 2, :], ACT.Copy,
                                           scale=ostat[:, t % 2, 2:3]).then_inc(on_s, 1)
                    if n is not None:
                        if s < SLOTS and s % 6 == 2:
                            j = s // 6 + 1
                            if j < UNITS:
                                split_high(n * UNITS + (1 + j), slot_of(j), landed_of(n, j))
                            elif not (isinstance(n, int) and n == H - 1):
                                split_high(n * UNITS + (1 + j), slot_of(0), landed_of(n + 1, 0))
                        q, k = divmod(s - 3, 3)
                        if 0 <= q < HALVES and k == 0:
                            half = q % 2
                            act.wait_ge(proj_mm, n * HALVES + (q + 3))
                            if q < 8:
                                act.wait_ge(convs, n * 8 + (q // 2 * 2 + 1))
                                act.activation(x_raw[:, CONV - 1 + half * HALF:CONV - 1 + (half + 1) * HALF],
                                               proj[half][:, :], ACT.Copy).then_inc(evac, 1)
                            else:
                                if q < 10:
                                    act.wait_ge(v_turned, n * 4 + (q - 5))
                                else:
                                    act.wait_ge(act_out, n * HALVES + (q - 1 + 2))
                                act.activation(acc[:, half], proj[half][:, :], ACT.Copy).then_inc(evac, 1)
                        q, k = divmod(s - 5, 3)
                        if 0 <= q < HALVES and k == 0:
                            act.wait_ge(arg, n * HALVES + (q + 1))
                            act.activation(sg[:, q % 2], sg[:, q % 2], ACT.Exp).then_inc(sigs, 1)
                            act.wait_ge(sigs, n * (2 * HALVES) + (2 * q + 1))
                            act.activation(sg[:, q % 2], sg[:, q % 2], ACT.Ln, bias=1.0).then_inc(sigs, 1)
                            act.wait_ge(sigs, n * (2 * HALVES) + (2 * q + 2))
                            act.activation(sg[:, q % 2], sg[:, q % 2], ACT.Exp, scale=-1.0).then_inc(sig, 1)
                        q, k = divmod(s - 7, 3)
                        if 0 <= q < 4 and k == 0:
                            act.wait_ge(act_out, n * HALVES + (q + 1 + 2))
                            act.activation(sg[:, q % 2], acc[:, q % 2], ACT.Square).then_inc(sq, 1)
                        q, k = divmod(s - 9, 3)
                        if 0 <= q < 4 and k == 0:
                            act.wait_ge(nsum, n * 4 + (q + 1))
                            act.activation(sg[:, q % 2], turn[:, :], ACT.Ln, bias=EPS).then_inc(rss, 1)
                            act.wait_ge(rss, n * 4 + (q + 1))
                            act.activation(sg[:, q % 2], sg[:, q % 2], ACT.Exp, scale=-0.5,
                                           bias=0.0 if q < 2 else -0.5 * float(np.log(DK))).then_inc(rs, 1)
                        if 4 <= q < 8 and k == 0:
                            act.wait_ge(v_turned, n * 4 + (q - 3))
                            c = q // 2 - 2
                            act.activation(v[:, p, (q % 2) * TH:(q % 2 + 1) * TH, c * P:(c + 1) * P],
                                           turn[:, :].rearrange("p (t c) -> p t c", t=TH),
                                           ACT.Copy).then_inc(v_kept, 1)
                        if s - 1 in DECAYS:
                            half = DECAYS.index(s - 1)
                            tiles = dec[:, half * TH:(half + 1) * TH, :]
                            act.wait_ge(darg, n * T + (half + 1) * TH)
                            act.activation(tiles, tiles, ACT.Exp).then_inc(dexp, 1)

            heads(act, body)

        @block.tensor
        def _(pe):
            pe.wait_ge(w_low, 1)
            for b in range(2):
                for third in range(3):
                    last = three_passes(pe, proj[b][:, :], w_hi[0], w_lo[0], g.h_hi, g.h_lo,
                                        slice(b * HALF, (b + 1) * HALF), third)
                last.then_inc(proj_mm, 1)
            pe.wait_ge(evac, 2)
            for t in range(T):
                last = pe.transpose(turn[:, t * 2 * H:(t + 1) * 2 * H], ba[:, t * P:(t + 1) * P],
                                    g.ident[0:2 * H, 0:2 * H])
            last.then_inc(setup, 1)
            pe.wait_ge(setup, 12)
            log = cols[:, C_LOG].rearrange("p t h -> p (t h)")
            pe.matmul(turn[:, 256:256 + T * H], g.tri[:, :], log, start=True, stop=True)
            pe.matmul(turn[:, 384:384 + T * H], g.ones[:, :], log, start=True, stop=True).then_inc(setup, 1)

            def body(m, n, p):
                pm = 1 - p
                order = turn_order(m is not None, n is not None)

                def turn_is_free(use):
                    i = order.index(use)
                    if i == 0:
                        if m is not None:
                            pe.wait_ge(og_s, m * T + T)
                            pe.wait_ge(v_kept, m * 4 + 4)
                        else:
                            pe.wait_ge(setup, 14)
                        return
                    what, c = order[i - 1]
                    if what == "o":
                        pe.wait_ge(og_s, m * T + (c + 1 + T))
                    if what == "sum":
                        pe.wait_ge(rss, n * 4 + (c + 1))
                    if what == "k":
                        pe.wait_ge(k_kept, n * 2 + (c + 1))
                    if what == "v":
                        pe.wait_ge(v_kept, n * 4 + (c + 1))

                for s in range(SLOTS):
                    if m is not None:
                        t, k = divmod(s - CHAIN0, 3)
                        if 0 <= t < T:
                            if k == 0:
                                pe.wait_ge(st_s, m * T + (t + 1))
                                pe.wait_ge(o_s, m * T + (t + 2))
                                for c in range(2):
                                    last = pe.matmul(step[:, c], kq[:, pm, t, c], state[:, t % 2, :],
                                                     start=True, stop=True)
                                last.then_inc(ks_mm, 1)
                            if k == 1:
                                pe.wait_ge(r_s, m * T + (t + 1))
                                if t % 2 == 0:
                                    pe.wait_ge(lv_s, m * (LEVELS * T // 2) + (LEVELS * (t // 2 + 1) + 1))
                                pe.wait_ge(vn_s, m * T + (t + 1))
                                pe.matmul(new[:, :], zf[:, t], r[:, :], start=True, stop=True).then_inc(xr_mm, 1)
                            if k == 2:
                                pe.wait_ge(vn_s, m * T + (t + 1 + 1))
                                pe.wait_ge(o1_s, m * T + (t + 1 + 1))
                                pe.matmul(step[:, 1], kd[:, t], vn[:, :], start=True, stop=True)
                                pe.matmul(step[:, 0], attn[:, pm, t], vn[:, :], start=True, stop=True
                                          ).then_inc(osu_mm, 1)
                        t, k = divmod(s - CHAIN0 - 6, 3)
                        if 0 <= t < T and k == 0:
                            pe.wait_ge(on_s, m * T + (t + 1))
                            turn_is_free(("o", t))
                            for c in range(VT):
                                last = pe.transpose(turn[:, c * P:(c + 1) * P], o[:, t % 2, c * P:(c + 1) * P],
                                                    g.ident[:, :])
                            last.then_inc(o_mm, 1)
                    if n is not None:
                        q, third = divmod(s, 3)
                        j, half = divmod(q, 2)
                        if third == 0:
                            pe.wait_ge(w_low, n * UNITS + (j + 2))
                            pe.wait_ge(evac, n * HALVES + (q + 1))
                        last = three_passes(pe, proj[half][:, :], w_hi[slot_of(j)], w_lo[slot_of(j)],
                                            g.h_hi, g.h_lo, slice(half * HALF, (half + 1) * HALF), third)
                        if third == 2:
                            last.then_inc(proj_mm, 1)
                        if s in (8, 11, 14, 17):
                            q = (s - 8) // 3
                            pe.wait_ge(sq, n * 4 + (q + 1))
                            turn_is_free(("sum", q))
                            pe.matmul(turn[:, :], g.ones[:, :], sg[:, q % 2], start=True, stop=True).then_inc(nsum, 1)
                        if s in K_TURNS:
                            half = K_TURNS.index(s)
                            pe.wait_ge(kqn, n * 4 + (half + 1))
                            turn_is_free(("k", half))
                            for t in range(TH):
                                last = pe.transpose(turn[:, t * P:(t + 1) * P], kq[:, p, half * TH + t, 0],
                                                    g.ident[:, :])
                            last.then_inc(k_turned, 1)
                        if s in (20, 23, 26, 29):
                            c = (s - 20) // 3
                            pe.wait_ge(act_out, n * HALVES + (4 + c + 1 + 2))
                            turn_is_free(("v", c))
                            for t in range(TH):
                                last = pe.transpose(turn[:, t * P:(t + 1) * P], acc[:, c % 2, t * P:(t + 1) * P],
                                                    g.ident[:, :])
                            last.then_inc(v_turned, 1)
                        if s in DECAYS:
                            half = DECAYS.index(s)
                            if half:
                                pe.wait_ge(darg, n * T + TH)
                            else:
                                pe.wait_ge(hc_s, n * 5 + 5)
                                if not (isinstance(n, int) and n == 0):
                                    pe.wait_ge(ut, n * (T // 2))
                            for t in range(TH):
                                last = pe.matmul(gram[:, t * P:(t + 1) * P], spread(hc[:, p, C_LOG, half * TH + t], 1, P),
                                                 g.tri[:, :], start=True, stop=True)
                            last.then_inc(row_mm, 1)
                        b, k = divmod(s - GRAM0, 2)
                        if 0 <= b < T // 2 and k == 0:
                            pe.wait_ge(kqn, n * 4 + (3 + b // 2))
                            if b:
                                pe.wait_ge(ut, n * (T // 2) + b)
                            else:
                                pe.wait_ge(darg, n * T + T)
                            for e in range(2):
                                last = pe.matmul(gram[:, e * 2 * P:(e + 1) * 2 * P], kq[:, p, 2 * b + e, 0],
                                                 kq[:, p, 2 * b + e, :, :].rearrange("p c i -> p (c i)"),
                                                 start=True, stop=True)
                            last.then_inc(gram_mm, 1)
                    if m is not None:
                        b, k = divmod(s - LEVEL0, 6)
                        if 0 <= b < T // 2:
                            level, second = divmod(k, 2)
                            use = LEVELS * b + level
                            x = zx[:, 2 * b:2 * b + 2] if level == 0 else zx1[:, :, :, :]
                            if not second:
                                if level:
                                    pe.wait_ge(lv_s, m * (LEVELS * T // 2) + (use + 1))
                                else:
                                    if b < 2:
                                        pe.wait_ge(back[b], m * 32 + 32)
                                    pe.wait_ge(um_s, m * (T // 2) + (b + 1))
                                for e in range(2):
                                    last = pe.matmul(first[:, e, :], um[:, e, level], x[:, e, 1], start=True, stop=True)
                                last.then_inc(first_mm, 1)
                            else:
                                pe.wait_ge(first_c, m * (LEVELS * T // 2) + (use + 1))
                                if level == 0:
                                    pe.wait_ge(lv_s, m * (LEVELS * T // 2) + (use + 1))
                                for e in range(2):
                                    last = pe.matmul(lev[:, e, 0], bc[:, e], x[:, e, 0], start=True, stop=True)
                                    if level < LEVELS - 1:
                                        last = pe.matmul(lev[:, e, 1], x[:, e, 0], bc[:, e], start=True, stop=True)
                                last.then_inc(lv_mm, 1)

            heads(pe, body)

        @block.vector
        def _(dve):
            def split_low(idx, slot):
                dve.wait_ge(w_high, idx + 1)
                dve.tensor_tensor(w_lo[slot][:, :, :], raw[:, slot], w_hi[slot][:, :, :].bitcast(F32),
                                  ALU.subtract).then_inc(w_low, 1)

            dve.memset(raw[:, 0], 0.0).then_inc(setup, 1)
            dve.memset(x_raw[:, 0:CONV - 1], 0.0).then_inc(convs, 1)
            dve.memset(state[:, 0, :], 0.0).then_inc(st_s, 1)
            dve.memset(state[:, 1, :], 0.0)
            for s_, c in ((act_out, 2), (o_s, 2), (og_s, T), (o1_s, 1), (vn_s, 1), (o_mm, 2),
                          (o_stored, 16),
                          (first_mm, 1), (osu_mm, 1), (lv_s, 1), (ostats, 6)):
                dve.sem_inc(s_, c)
            split_low(0, 0)
            split_low(1, 1)
            dve.wait_ge(setup, 2)
            logits = turn[:, 0:T * 2 * H].rearrange("p (t h) -> p t h", t=T)
            dve.tensor_scalar(tmp[:, 0], logits[:, :, 0:H], -1.0, ARG_MAX, ALU.mult, ALU.min)
            dve.tensor_tensor(tmp[:, 1], logits[:, :, H:2 * H], spread(g.head_bc[:, H:2 * H], 1, T),
                              ALU.add).then_inc(setup, 1)
            dve.wait_ge(setup, 10)
            dve.scalar_tensor_tensor(tmp[:, 2], tmp[:, 1], 0.0, tmp[:, 2], ALU.max, ALU.add).then_inc(setup, 1)
            dve.wait_ge(setup, 11)
            dve.scalar_tensor_tensor(cols[:, C_LOG], tmp[:, 2], -1.0, spread(neg_a[:, :], 1, T),
                                     ALU.mult, ALU.mult).then_inc(setup, 1)
            dve.wait_ge(setup, 13)
            cum = turn[:, 256:256 + T * H].rearrange("p (t h) -> p t h", t=T)
            total = turn[:, 384:384 + T * H].rearrange("p (t h) -> p t h", t=T)
            dve.tensor_copy(cols[:, C_CUM], cum)
            dve.tensor_copy(tmp[:, 0], total).then_inc(totals, 1)
            dve.wait_ge(totals, 1)
            dve.tensor_tensor(tmp[:, 1], tmp[:, 0], cols[:, C_CUM], ALU.subtract).then_inc(setup, 1)
            dve.wait_ge(setup, 17)
            dve.tensor_scalar(cols[:, C_NEXP], cols[:, C_EXP], -1.0, None, ALU.mult).then_inc(cols_s, 1)

            def body(m, n, p):
                pm = 1 - p
                for s in range(DELAYED):
                    if m is not None:
                        b, k = divmod(s - LEVEL0 - 2, 6)
                        if 0 <= b < T // 2 and k % 2 == 0:
                            level = k // 2
                            use = LEVELS * b + level
                            x = zx[:, 2 * b:2 * b + 2] if level == 0 else zx1[:, :, :, :]
                            dve.wait_ge(lv_mm, m * (LEVELS * T // 2) + (use + 1))
                            if level:
                                dve.wait_ge(lv_s, m * (LEVELS * T // 2) + (use + 1))
                            if level < LEVELS - 1:
                                dve.tensor_tensor(zx1[:, :, :, :], x, lev[:, :, :, :], ALU.subtract).then_inc(lv_s, 1)
                            else:
                                dve.tensor_tensor(zf[:, 2 * b:2 * b + 2, :], x[:, :, 0], lev[:, :, 0],
                                                  ALU.subtract).then_inc(lv_s, 1)
                        t, k = divmod(s - CHAIN0, 3)
                        if 0 <= t < T and k == 0:
                            dve.wait_ge(ks_mm, m * T + (t + 1))
                            dve.scalar_tensor_tensor(r[:, :], step[:, 0], hc[:, pm, C_NEXP, t:t + 1], v[:, pm, t, :],
                                                     ALU.mult, ALU.add).then_inc(r_s, 1)
                        if 0 <= t < T and k == 2:
                            dve.wait_ge(osu_mm, m * T + (t + 1 + 1))
                            dve.wait_ge(st_s, m * T + (t + 1))
                            if t == T - 1:
                                dve.memset(state[:, 0, :], 0.0).then_inc(st_s, 1)
                            else:
                                dve.scalar_tensor_tensor(state[:, (t + 1) % 2, :], state[:, t % 2, :],
                                                         hc[:, pm, C_LAST, t:t + 1], step[:, 1],
                                                         ALU.mult, ALU.add).then_inc(st_s, 1)
                            dve.wait_ge(o1_s, m * T + (t + 2))
                            dve.wait_ge(o_mm, m * T + (t - 1 + 2))
                            dve.tensor_tensor(o[:, t % 2, :], step[:, 0], o1[:, t % 2, :], ALU.add).then_inc(o_s, 1)
                        t, k = divmod(s - CHAIN0 - 6, 3)
                        if 0 <= t < T and k == 0:
                            dve.wait_ge(o_mm, m * T + (t + 1 + 2))
                            dve.wait_ge(o_stored, m * (16 * T) + 16 * (t + 1))
                            dve.tensor_tensor(og[:, :, :], turn[:, 0:DV].rearrange("p (c i) -> p c i", c=VT),
                                              z[:, pm, :, t * P:(t + 1) * P], ALU.mult).then_inc(og_s, 1)
                    if n is not None:
                        if s < SLOTS and s % 6 == 3:
                            j = s // 6 + 1
                            if j < UNITS or not (isinstance(n, int) and n == H - 1):
                                split_low(n * UNITS + (1 + j), slot_of(j % UNITS))
                        if s == 4:
                            dve.wait_ge(hc_s, n * 5 + 5)
                        q, k = divmod(s - 10, 3)
                        if 0 <= q < 4 and k == 0:
                            dve.wait_ge(rs, n * 4 + (q + 1))
                            dve.tensor_tensor(kq[:, p, (q % 2) * TH:(q % 2 + 1) * TH, q // 2, :],
                                              acc[:, q % 2].rearrange("p (t i) -> p t i", t=TH),
                                              sg[:, q % 2].rearrange("p (t i) -> p t i", t=TH),
                                              ALU.mult).then_inc(kqn, 1)
                        q, k = divmod(s - 4, 3)
                        if 0 <= q < HALVES and k == 0:
                            half, j = q % 2, q // 2
                            dve.wait_ge(act_out, n * HALVES + (q - 1 + 2))
                            if 2 <= q < 6:
                                dve.wait_ge(kqn, n * 4 + (q - 1))
                            dve.wait_ge(evac, n * HALVES + (q + 3))
                            if q in (6, 7):
                                dve.wait_ge(v_turned, n * 4 + (q - 5))
                            if q < 8:
                                for tap in range(CONV):
                                    if tap:
                                        dve.wait_ge(taps, n * 24 + (3 * q + tap))
                                    src = x_raw[:, half * HALF + tap:half * HALF + tap + HALF]
                                    w = hw[:, p, tap, j:j + 1]
                                    if tap == 0:
                                        ins = dve.tensor_scalar(acc[:, half], src, w, None, ALU.mult)
                                    else:
                                        ins = dve.scalar_tensor_tensor(acc[:, half], src, w, acc[:, half],
                                                                       ALU.mult, ALU.add)
                                    ins.then_inc(taps if tap < CONV - 1 else convs, 1)
                                dve.wait_ge(convs, n * 8 + (q + 2))
                            dve.tensor_scalar(sg[:, half], acc[:, half], -1.0, ARG_MAX, ALU.mult,
                                              ALU.min).then_inc(arg, 1)
                        q, k = divmod(s - 6, 3)
                        if 0 <= q < HALVES and k == 0:
                            half = q % 2
                            dve.wait_ge(sig, n * HALVES + (q + 1))
                            if q < 8:
                                dve.tensor_tensor(acc[:, half], acc[:, half], sg[:, half], ALU.mult).then_inc(act_out, 1)
                            else:
                                c = q // 2 - 4
                                dve.wait_ge(og_s, n * T)
                                dve.scalar_tensor_tensor(z[:, p, c, half * HALF:(half + 1) * HALF], acc[:, half],
                                                         g.gains[:, 16 + c:17 + c], sg[:, half],
                                                         ALU.mult, ALU.mult).then_inc(act_out, 1)
                        if s in K_TURNS:
                            half = K_TURNS.index(s)
                            tiles = slice(half * TH, (half + 1) * TH)
                            dve.wait_ge(k_turned, n * 2 + (half + 1))
                            if m is not None:
                                dve.wait_ge(osu_mm, m * T + ((half + 1) * TH + 1))
                            dve.tensor_tensor(kd[:, tiles, :], turn[:, :].rearrange("p (t c) -> p t c", t=TH),
                                              spread(hc[:, p, C_TAIL, tiles], 2, P), ALU.mult).then_inc(k_kept, 1)
                        b, k = divmod(s - GRAM0 - 1, 2)
                        if 0 <= b < T // 2 and k == 0:
                            dve.wait_ge(gram_mm, n * (T // 2) + (b + 1))
                            dve.wait_ge(dexp, n * 2 + (b // 2 + 1))
                            if not (isinstance(n, int) and n == 0):
                                dve.wait_ge(blocks_out, n * 16)
                            if m is not None:
                                dve.wait_ge(um_s, m * (T // 2) + (b + 1))
                            pair = gram[:, :].rearrange("p (e c i) -> p e c i", e=2, c=2)
                            for e in range(2):
                                t = 2 * b + e
                                dve.scalar_tensor_tensor(u[:, t], pair[:, e, 0], hc[:, p, C_BETA, t:t + 1], dec[:, t],
                                                         ALU.mult, ALU.mult)
                            dve.tensor_tensor(attn[:, p, 2 * b:2 * b + 2], pair[:, :, 1], dec[:, 2 * b:2 * b + 2],
                                              ALU.mult).then_inc(ut, 1)
                        if s in DECAYS:
                            half = DECAYS.index(s)
                            dve.wait_ge(row_mm, n * 2 + (half + 1))
                            for t in range(TH):
                                at = half * TH + t
                                dve.scalar_tensor_tensor(dec[:, at], gram[:, t * P:(t + 1) * P],
                                                         hc[:, p, C_CUM, at:at + 1], g.decay_mask[:, :],
                                                         ALU.subtract, ALU.add).then_inc(darg, 1)

            heads(dve, body)


def out_projection(nc, tag, o_turned, w, x_in, x_out, k_tiles):
    RING = 4
    GROUPS = k_tiles // RING
    with ExitStack() as ctx:
        m = Mem(nc, ctx, tag)
        w_raw = m.sb("w_raw", [P, RING, D])
        a_raw = m.sb("a_raw", [P, RING, HALF])
        w_hi = [m.sb(f"w_hi{i}", [P, D], F32R) for i in range(RING)]
        w_lo = [m.sb(f"w_lo{i}", [P, D], F32R) for i in range(RING)]
        a_hi = [m.sb(f"a_hi{i}", [P, HALF], F32R) for i in range(RING)]
        a_lo = [m.sb(f"a_lo{i}", [P, HALF], F32R) for i in range(RING)]
        x = m.sb("x", [P, 2, TH, D])
        y = [m.ps(f"y{i}", [P, HALF]) for i in range(2 * TH)]
        landed = [m.sem(f"landed{i}") for i in range(RING)]
        x_landed = [m.sem("x_landed0"), m.sem("x_landed1")]
        high, low = m.sem("high"), m.sem("low")
        used = m.sem("used")
        summed = m.sem("summed")
        stored = m.sem("stored")
        block = ctx.enter_context(nc.Block())

        def units(eng, unit, between=None):
            for half in range(2):
                unit(half, 0, True, False)
                if GROUPS > 2:
                    with eng.Fori(1, GROUPS - 1) as i:
                        unit(half, i, False, False)
                unit(half, GROUPS - 1, False, True)
                if between:
                    between(half)

        def index(half, i, c):
            return half * k_tiles + i * RING + c

        @block.sync
        def _(sp):
            def load(half, i, first, last):
                for c in range(RING):
                    if not (first and half == 0):
                        sp.wait_ge(low, index(half, i, c) + (1 - RING))
                    row = i * (RING * P) + c * P
                    sp.dma_start(w_raw[:, c, :], w[bass.ds(row, P), :]).then_inc(landed[c], 16)
                    sp.dma_start(a_raw[:, c, :], o_turned[bass.ds(row, P), half * HALF:(half + 1) * HALF]
                                 ).then_inc(landed[c], 16)
                if first:
                    sp.dma_start(x[:, half], x_in[half * HALF:(half + 1) * HALF, :]
                                 .rearrange("(t p) n -> p t n", p=P)).then_inc(x_landed[half], 16)

            units(sp, load)
            for half in range(2):
                for t in range(TH):
                    sp.wait_ge(summed, half * 2 * TH + 2 * t + 2)
                    row = half * HALF + t * P
                    sp.dma_start(x_out[row:row + P, :], x[:, half, t, :]).then_inc(stored, 16)
            sp.wait_ge(stored, 16 * T)

        @block.scalar
        def _(act):
            def split(half, i, first, last):
                for c in range(RING):
                    act.wait_ge(landed[c], i * 32 + (half * GROUPS * 32 + 32))
                    if not (first and half == 0):
                        act.wait_ge(used, index(half, i, c) + (1 - RING))
                    act.activation(a_hi[c][:, :], a_raw[:, c, :], ACT.Copy).then_inc(high, 1)
                    act.activation(w_hi[c][:, :], w_raw[:, c, :], ACT.Copy).then_inc(high, 1)
            units(act, split)

        @block.vector
        def _(dve):
            def split(half, i, first, last):
                for c in range(RING):
                    dve.wait_ge(high, (i * RING + half * k_tiles + c) * 2 + 2)
                    dve.tensor_tensor(a_lo[c][:, :], a_raw[:, c, :], a_hi[c][:, :].bitcast(F32), ALU.subtract)
                    dve.tensor_tensor(w_lo[c][:, :], w_raw[:, c, :], w_hi[c][:, :].bitcast(F32),
                                      ALU.subtract).then_inc(low, 1)

            def add(half):
                dve.wait_ge(x_landed[half], 16)
                dve.wait_ge(used, (half + 1) * k_tiles)
                for b in range(2 * TH):
                    cell = x[:, half, b // 2, (b % 2) * HALF:(b % 2 + 1) * HALF]
                    dve.tensor_tensor(cell, y[b][:, :], cell, ALU.add).then_inc(summed, 1)
            units(dve, split, add)

        @block.tensor
        def _(pe):
            def multiply(half, i, first, last):
                for c in range(RING):
                    pe.wait_ge(low, index(half, i, c) + 1)
                    for b in range(2 * TH):
                        if first and half and c == 0:
                            pe.wait_ge(summed, b + 1)
                        ts = slice((b // 2) * P, (b // 2 + 1) * P)
                        ns = slice((b % 2) * HALF, (b % 2 + 1) * HALF)
                        for n, (a_, w_) in enumerate(((a_hi, w_hi), (a_hi, w_lo), (a_lo, w_hi))):
                            mm = pe.matmul(y[b][:, :], a_[c][:, ts], w_[c][:, ns],
                                           start=(first and c == 0 and n == 0),
                                           stop=(last and c == RING - 1 and n == 2))
                    mm.then_inc(used, 1)
            units(pe, multiply)


B_UNITS = 3 * NG + 1
B_HALVES = 2 * B_UNITS
B_SLOTS = 3 * B_HALVES
B_DELAYED = B_SLOTS + 6
SCORE = DK ** -0.5
PAIRS = 12
BATCHES = 9
BATCH0 = 25


def rope_tables(nc, tag, r, positions):
    TWO_PI = 2.0 * np.pi
    part1 = 6.28125
    part2 = float(np.float32(np.round((TWO_PI - part1) * 2.0 ** 20) / 2.0 ** 20))
    part3 = float(np.float32(TWO_PI - part1 - part2))
    ROUND = 1.5 * 2.0 ** 23
    PI = float(np.float32(3.1415925))
    freq = (np.float32(THETA) ** (-np.arange(0, ROPE, 2, dtype=np.float32) / np.float32(ROPE))).astype(np.float32)
    with ExitStack() as ctx:
        m = Mem(nc, ctx, tag)
        pos = m.sb("pos", [ROPE, S], I32)
        ang = m.sb("ang", [ROPE, S])
        turns = m.sb("turns", [ROPE, S])
        rest = m.sb("rest", [ROPE, S])
        row = m.sb("row", [1, 2 * ROPE])
        sign_row = m.sb("sign_row", [1, P])
        col = m.sb("col", [ROPE, 2])
        ps = m.ps("ps", [P, 512])
        landed, made, turned, step, sines = (m.sem(x) for x in ("landed", "made", "turned", "step", "sines"))
        block = ctx.enter_context(nc.Block())

        @block.sync
        def _(sp):
            sp.dma_start(pos[:, :], positions.partition_broadcast(ROPE)).then_inc(landed, 16)

        @block.gpsimd
        def _(pool):
            for i in range(HR):
                pool.memset(row[:, i:i + HR + 1:HR], float(freq[i])).then_inc(made, 1)
            pool.memset(row[:, ROPE:ROPE + HR], -1.0).then_inc(made, 1)
            pool.memset(row[:, ROPE + HR:], 1.0).then_inc(made, 1)
            pool.memset(sign_row[:, 0::2], 1.0).then_inc(made, 1)
            pool.memset(sign_row[:, 1::2], -1.0).then_inc(made, 1)
            pool.memset(r.band_mask[:, :], 0.0).then_inc(made, 1)
            pool.wait_ge(made, HR + 5)
            pool.affine_select(out=r.band_mask[:, 0:P], in_=r.band_mask[:, 0:P], compare_op=ALU.is_ge, fill=-BIG,
                               base=0, pattern=[[1, P]], channel_multiplier=-1).then_inc(made, 1)
            pool.affine_select(out=r.band_mask[:, P:], in_=r.band_mask[:, P:], compare_op=ALU.is_ge, fill=-BIG,
                               base=0, pattern=[[-1, P]], channel_multiplier=1).then_inc(made, 1)
            pool.wait_ge(step, 1)
            pool.affine_select(out=r.pair_mask[:, :], in_=r.pair_mask[:, :], compare_op=ALU.is_ge, fill=-BIG,
                               base=0, pattern=[[-1, P]], channel_multiplier=1).then_inc(made, 1)
            pool.wait_ge(made, HR + 8)

        @block.tensor
        def _(pe):
            pe.wait_ge(made, HR + 4)
            pe.matmul(ps[0:ROPE, 0:1], row[:, 0:ROPE], r.ones[0:1, 0:1], start=True, stop=True)
            pe.matmul(ps[0:ROPE, 1:2], row[:, ROPE:], r.ones[0:1, 0:1], start=True, stop=True)
            pe.matmul(ps[:, 128:256], sign_row[:, :], sign_row[:, :], start=True, stop=True).then_inc(turned, 1)

        @block.vector
        def _(dve):
            steps = []

            def chained(ins):
                steps.append(ins)
                ins.then_inc(step, 1)
                dve.wait_ge(step, len(steps))

            dve.wait_ge(turned, 1)
            chained(dve.tensor_scalar(r.pair_mask[:, :], ps[:, 128:256], -1.0, BIG / 2, ALU.add, ALU.mult))
            chained(dve.tensor_copy(col[:, :], ps[0:ROPE, 0:2]))
            dve.wait_ge(landed, 16)
            chained(dve.tensor_copy(ang[:, :], pos[:, :]))
            chained(dve.tensor_scalar(ang[:, :], ang[:, :], col[:, 0:1], None, ALU.mult))
            for n, (out, shift) in enumerate(((r.sin, 0.0), (r.cos, 0.25))):
                chained(dve.tensor_scalar(turns[:, :], ang[:, :], 1.0 / TWO_PI, shift, ALU.mult, ALU.add))
                chained(dve.tensor_scalar(turns[:, :], turns[:, :], ROUND, None, ALU.add))
                chained(dve.tensor_scalar(turns[:, :], turns[:, :], ROUND, None, ALU.subtract))
                if n:
                    dve.wait_ge(sines, 1)
                chained(dve.scalar_tensor_tensor(rest[:, :], turns[:, :], -part1, ang[:, :], ALU.mult, ALU.add))
                chained(dve.scalar_tensor_tensor(rest[:, :], turns[:, :], -part2, rest[:, :], ALU.mult, ALU.add))
                chained(dve.scalar_tensor_tensor(rest[:, :], turns[:, :], -part3, rest[:, :], ALU.mult, ALU.add))
                chained(dve.tensor_scalar(rest[:, :], rest[:, :], shift * TWO_PI, PI, ALU.add, ALU.min))
                chained(dve.tensor_scalar(rest[:, :], rest[:, :], -PI, None, ALU.max))
            dve.wait_ge(sines, 2)
            chained(dve.tensor_scalar(r.sin[:, :], r.sin[:, :], col[:, 1:2], None, ALU.mult))

        @block.scalar
        def _(act):
            for n, out in enumerate((r.sin, r.cos)):
                act.wait_ge(step, 12 + 8 * n)
                act.activation(out[:, :], rest[:, :], ACT.Sin).then_inc(sines, 1)


def attention_heads(nc, r, b_w_in, positions, o_turned):
    with ExitStack() as ctx:
        m_ = Mem(nc, ctx, "b")
        r.cos = m_.sb("cos", [ROPE, S])
        r.sin = m_.sb("sin", [ROPE, S])
        r.band_mask = m_.sb("band_mask", [P, 2 * P])
        r.pair_mask = m_.sb("pair_mask", [P, P])
        rope_tables(nc, "t", r, positions)

        raw = m_.sb("raw", [P, 2, KD, P])
        w_hi = [m_.sb(f"w_hi{i}", [P, KD, P], F32R) for i in range(2)]
        w_lo = [m_.sb(f"w_lo{i}", [P, KD, P], F32R) for i in range(2)]
        qk = m_.sb("qk", [P, 2 * NG, S])
        v_raw = m_.sb("v_raw", [P, S])
        v = m_.sb("v", [P, NG, T, P])
        sc = m_.sb("sc", [P, 36 * P])
        kept = m_.sb("kept", [P, 2, 4, P])
        pairs_kept = m_.sb("pairs_kept", [P, T, P])
        acc = m_.sb("acc", [P, 2, HALF])
        sg = m_.sb("sg", [P, 2, HALF])
        swap = m_.sb("swap", [ROPE, HALF])
        z = m_.sb("z", [P, S])
        zl = m_.sb("zl", [P, S])
        fin = m_.sb("fin", [P, 2, HALF])
        og = m_.sb("og", [P, HALF])
        mx = m_.sb("mx", [P, NG, T])
        mo = m_.sb("mo", [P, 2, T])
        nb = m_.sb("nb", [P, NG, T])
        mx_dram = nc.dram_tensor("maxima", [3, S], F32, kind="Internal").ap()

        proj = [m_.ps(f"proj{i}", [P, HALF]) for i in range(2)]
        side = m_.ps("side", [P, HALF])
        ring = [m_.ps(f"ring{i}", [P, HALF]) for i in range(3)]
        num = m_.ps("num", [P, HALF])
        den = m_.ps("den", [P, HALF])

        sem = m_.sem
        w_landed = [sem("w_landed0"), sem("w_landed1")]
        w_high, w_low = sem("w_high"), sem("w_low")
        proj_mm, evac, squares = sem("proj_mm"), sem("evac"), sem("squares")
        nsum, rss, rs = sem("nsum"), sem("rss"), sem("rs")
        rope, ropes, qkn = sem("rope"), sem("ropes"), sem("qkn")
        v_turned, v_kept = sem("v_turned"), sem("v_kept")
        zarg, zexp, zln = sem("zarg"), sem("zexp"), sem("zln")
        score_mm, mxs = sem("score_mm"), sem("mxs")
        mx_out, mx_in, mmax, mcol = sem("mx_out"), sem("mx_in"), sem("mmax"), sem("mcol")
        nb_out, nb_in, nbs = sem("nb_out"), sem("nb_in"), sem("nbs")
        exps = sem("exps")
        p_turned, p_kept = sem("p_turned"), [sem("p_kept0"), sem("p_kept1")]
        pv = sem("pv")
        half_mm, lden, larg, lexp, nzr, ogs = (sem(x) for x in ("half_mm", "lden", "larg", "lexp", "nzr", "ogs"))
        o_stored = sem("o_stored")
        carrier = sem("carrier")
        block = ctx.enter_context(nc.Block())

        def col_of(n, j):
            if j < 2 * NG:
                return n * P + ((j % 2) * NG + j // 2) * D
            return n * P + j * D

        def slot_of(j):
            return j % 2

        def landed_of(n, j):
            return 16 * (n * (B_UNITS // 2) + j // 2 + 1)

        score_tiles = []
        at = 0
        for g, tile in [(0, i) for i in range(T)] + [(1, i) for i in range(T)] + [(2, i) for i in range(T)]:
            before = (g == 0 and tile > 0) or (g == 1 and tile >= TH)
            if g == 1:
                first = (tile % TH) * (2 * P) + (tile // TH) * P
            else:
                first = tile * P
            width = 2 * P if before else P
            score_tiles.append((g, tile, at, first, width, before))
            at += width
        assert at <= 36 * P
        tile_at = {(g, tile): (at, before) for g, tile, at, _, _, before in score_tiles}
        order = ([(0, i) for i in range(TH)] + [(1, i) for i in range(TH)] + [(2, i) for i in range(T)]
                 + [(0, i) for i in range(TH, T)] + [(1, i) for i in range(TH, T)])

        def out_cols(g, tile):
            if g == 0:
                return slice((tile % TH) * P, (tile % TH + 1) * P)
            return slice(tile % TH, HALF, TH) if g == 1 else slice(tile, HALF, T)

        def key_tile(g, tile, prev):
            return tile - (1 if g == 0 else TH) if prev else tile

        batches = [
            [(0, i, False) for i in range(0, TH)], [(0, i, True) for i in range(1, TH)],
            [(1, i, False) for i in range(0, TH)],
            [(2, i, False) for i in range(0, 4)], [(2, i, False) for i in range(4, T)],
            [(0, i, False) for i in range(TH, T)], [(0, i, True) for i in range(TH, T)],
            [(1, i, False) for i in range(TH, T)], [(1, i, True) for i in range(TH, T)],
        ]
        assert len(batches) == BATCHES
        RINGS = PAIRS + BATCHES

        def heads(eng, body):
            body(None, 0)
            with eng.Fori(0, H - 1) as i:
                body(i, i + 1)
            body(H - 1, None)

        def some(n):
            return not (isinstance(n, int) and n == 0)

        V_TURNS = tuple(3 * (13 + 2 * g) + 4 + c for g in range(NG) for c in range(2))

        def keep_batch(eng, m, i):
            eng.wait_ge(p_turned, m * BATCHES + (i + 1))
            eng.wait_ge(pv, m * (BATCHES + 1) + max(i - 1, 0) + 1)
            n = len(batches[i])
            if batches[i][0][0] == 2:
                out = pairs_kept[:, batches[i][0][1]:batches[i][0][1] + n, :]
            else:
                out = kept[:, i % 2, 0:n, :]
            src = ring[(PAIRS + i) % 3][:, 0:n * P].rearrange("p (t c) -> p t c", t=n)
            if eng.engine == nc.scalar.engine:
                eng.activation(out, src, ACT.Copy).then_inc(p_kept[i % 2], 1)
            else:
                eng.tensor_copy(out, src).then_inc(p_kept[i % 2], 1)

        def kept_count(m, i):
            return m * (BATCHES - BATCHES // 2 if i % 2 == 0 else BATCHES // 2) + i // 2 + 1

        @block.sync
        def _(sp):
            def load(n, j, first=False):
                if not first:
                    sp.wait_ge(w_low, n * B_UNITS + (j - 1))
                sp.dma_start(raw[:, slot_of(j)], b_w_in[:, bass.ds(col_of(n, j), P)]
                             .rearrange("(k p) c -> p k c", p=P)).then_inc(w_landed[slot_of(j)], 16)

            load(0, 0, True)
            load(0, 1, True)

            def body(m, n):
                last = isinstance(n, int) and n == H - 1
                for s in range(B_DELAYED):
                    if m is not None and s == 12:
                        sp.wait_ge(mxs, m * NG * T + NG * T)
                        sp.dma_start(mx_dram[0].rearrange("(t p) -> p t", p=P), mx[:, 0, :],
                                     allow_slow_non_contiguous=True).then_inc(mx_out, 16)
                        sp.dma_start(mx_dram[1].rearrange("(b p r) -> p b r", b=2, r=TH),
                                     mx[:, 1, :].rearrange("p (b r) -> p b r", b=2)).then_inc(mx_out, 16)
                        sp.wait_ge(mx_out, m * 32 + 32)
                        for c in range(2):
                            sp.dma_start(mo[:, c, :], mx_dram[c].rearrange("(p j) -> p j", j=T)).then_inc(mx_in, 16)
                    if m is not None and s == 17:
                        sp.wait_ge(nbs, m + 1)
                        sp.dma_start(mx_dram[2].rearrange("(p j) -> p j", j=T), nb[:, 2, :]).then_inc(nb_out, 16)
                        sp.wait_ge(nb_out, m * 16 + 16)
                        sp.dma_start(nb[:, 0, :], mx_dram[2].rearrange("(t p) -> p t", p=P),
                                     allow_slow_non_contiguous=True).then_inc(nb_in, 16)
                        sp.dma_start(nb[:, 1, :].rearrange("p (b r) -> p b r", b=2),
                                     mx_dram[2].rearrange("(b p r) -> p b r", b=2, r=TH)).then_inc(nb_in, 16)
                    if n is not None and s < B_SLOTS and s % 6 == 3:
                        j = s // 6 + 2
                        if j < B_UNITS:
                            load(n, j)
                        elif not last:
                            load(n + 1, j - B_UNITS)
                    if m is not None and s in (BATCH0 + 14, BATCH0 + 24):
                        half = (s - BATCH0 - 14) // 10
                        sp.wait_ge(ogs, m * 2 + (half + 1 + 2))
                        sp.dma_start(o_turned[bass.ds(m * P, P), half * HALF:(half + 1) * HALF], og[:, :]
                                     ).then_inc(o_stored, 16)

            heads(sp, body)
            sp.wait_ge(o_stored, 16 * (1 + 2 * H))

        @block.scalar
        def _(act):
            def split_high(n, j, first=False):
                act.wait_ge(w_landed[slot_of(j)], landed_of(n, j))
                if not first:
                    act.wait_ge(proj_mm, n * B_HALVES + (2 * j - 2))
                act.activation(w_hi[slot_of(j)][:, :, :], raw[:, slot_of(j)], ACT.Copy).then_inc(w_high, 1)

            act.preload_act_table_set(EXP_LN)
            split_high(0, 0, True)

            def body(m, n):
                last = isinstance(n, int) and n == H - 1
                for s in range(B_DELAYED):
                    if m is not None:
                        if 22 <= s < 34:
                            if s == 22:
                                act.wait_ge(nb_in, m * 32 + 32)
                            for g, tile in order[2 * (s - 22):2 * (s - 22) + 2]:
                                at, before = tile_at[g, tile]
                                cell = sc[:, at:at + (2 * P if before else P)]
                                act.activation(cell, cell, ACT.Exp, scale=SCORE,
                                               bias=nb[:, g, tile:tile + 1]).then_inc(exps, 1)
                        i, k = divmod(s - BATCH0 - 1, 2)
                        if k == 0 and 0 <= i < BATCHES and i % 2 == 0:
                            keep_batch(act, m, i)
                        if s in (BATCH0 + 12, BATCH0 + 22):
                            half = (s - BATCH0 - 12) // 10
                            act.wait_ge(half_mm, m * 2 + (half + 1))
                            act.wait_ge(ogs, m * 2 + (half + 2))
                            act.activation(fin[:, 0], den[:, :], ACT.Ln).then_inc(lden, 1)
                            act.wait_ge(larg, m * 2 + (half + 1))
                            act.activation(fin[:, 0], fin[:, 0], ACT.Exp, scale=-1.0).then_inc(lexp, 1)
                    if n is not None:
                        if s < B_SLOTS and s % 6 == 2:
                            j = s // 6 + 1
                            if j < B_UNITS:
                                split_high(n, j, not some(n) and j == 1)
                            elif not last:
                                split_high(n + 1, 0)
                        q, k = divmod(s - 3, 3)
                        if k == 0 and 0 <= q < B_HALVES:
                            half, j = q % 2, q // 2
                            act.wait_ge(proj_mm, n * B_HALVES + (q + 1))
                            if j < 2 * NG:
                                act.wait_ge(qkn, n * 12 + (q - 1 + 2))
                                gain = 18 + (j % 2) * NG + j // 2
                                act.activation(acc[:, half], proj[half][:, :], ACT.Copy,
                                               scale=r.gains[:, gain:gain + 1]).then_inc(rope, 1)
                                act.activation(sg[:, half], proj[half][:, :], ACT.Square).then_inc(evac, 1)
                            elif j < 3 * NG:
                                act.wait_ge(v_turned, n * 6 + (2 * (j - 2 * NG) + 2))
                                act.activation(v_raw[:, half * HALF:(half + 1) * HALF], proj[half][:, :],
                                               ACT.Copy).then_inc(evac, 1)
                            else:
                                act.wait_ge(ogs, n * 2 + 2)
                                act.activation(z[:, half * HALF:(half + 1) * HALF], proj[half][:, :],
                                               ACT.Copy).then_inc(evac, 1)
                        q, k = divmod(s - 5, 3)
                        if k == 0 and 0 <= q < 12:
                            act.wait_ge(nsum, n * 12 + (q + 1))
                            act.activation(sg[:, q % 2], side[:, :], ACT.Ln, scale=1.0 / DK, bias=EPS).then_inc(rss, 1)
                            act.wait_ge(rss, n * 12 + (q + 1))
                            act.activation(sg[:, q % 2], sg[:, q % 2], ACT.Exp, scale=-0.5).then_inc(rs, 1)
                        if k == 0 and q >= B_HALVES - 2 and q < B_HALVES:
                            half = q % 2
                            cell = zl[:, half * HALF:(half + 1) * HALF]
                            act.wait_ge(zarg, n * 2 + (half + 1))
                            act.activation(cell, cell, ACT.Exp).then_inc(zexp, 1)
                            act.wait_ge(zexp, n * 2 + (half + 1))
                            act.activation(cell, cell, ACT.Ln, bias=1.0).then_inc(zln, 1)
                        if s in V_TURNS:
                            c = V_TURNS.index(s)
                            act.wait_ge(v_turned, n * 6 + (c + 1 + 2))
                            act.activation(v[:, c // 2, (c % 2) * TH:(c % 2 + 1) * TH, :],
                                           side[:, :].rearrange("p (t c) -> p t c", t=TH), ACT.Copy).then_inc(v_kept, 1)

            heads(act, body)

        @block.tensor
        def _(pe):
            def multiply_batch(m, i):
                half = 0 if i < 5 else 1
                if i in (0, 5):
                    pe.wait_ge(nzr, m * 2 + (half + 1))
                    pe.wait_ge(lden, m * 2 + (half + 1))
                pe.wait_ge(p_kept[i % 2], kept_count(m, i) + 1)
                for c, (g, tile, prev) in enumerate(batches[i]):
                    if g == 2:
                        a, keys = pairs_kept[0:64, tile, 0:64], slice(0, 64)
                    else:
                        a, keys = kept[:, i % 2, c, :], slice(0, P)
                    cols = out_cols(g, tile)
                    start = i in (0, 5) and c == 0
                    stop = i == 4 and c == 3
                    pe.matmul(num[:, cols], v[keys, g, key_tile(g, tile, prev), :], a, start=start, stop=stop,
                              skip_group_check=True)
                    mm = pe.matmul(den[:, cols], r.ones[keys, :], a, start=start, stop=stop, skip_group_check=True)
                mm.then_inc(pv, 1)
                if i == 4:
                    pe.wait_ge(pv, m * (BATCHES + 1) + (5 + 1))
                    pe.sem_inc(half_mm, 1)

            def multiply_pairs(m):
                for j in range(T):
                    pe.matmul(num[:, out_cols(2, j)], v[:, 2, j, :], pairs_kept[:, j, 64:P], start=False,
                              stop=(j == T - 1), skip_group_check=True)
                    mm = pe.matmul(den[:, out_cols(2, j)], r.ones[:, :], pairs_kept[:, j, 64:P], start=False,
                                   stop=(j == T - 1), skip_group_check=True)
                mm.then_inc(pv, 1)
                pe.wait_ge(pv, m * (BATCHES + 1) + (BATCHES + 1 + 1))
                pe.sem_inc(half_mm, 1)

            def body(m, n):
                for s in range(B_SLOTS):
                    if m is not None:
                        if s < PAIRS:
                            if s == 0:
                                pe.wait_ge(qkn, m * 12 + 12 + 2)
                            if s < 3:
                                pe.wait_ge(p_kept[0], m * 5 + 1)
                                pe.wait_ge(p_kept[1], m * 4 + 1)
                            else:
                                pe.wait_ge(mxs, m * (NG * T) + 2 * (s - 2))
                            for c in range(2):
                                g, tile, at, first, width, before = score_tiles[2 * s + c]
                                begin = first - P if before else first
                                mm = pe.matmul(ring[s % 3][:, c * 2 * P:c * 2 * P + width],
                                               qk[:, 2 * g, first:first + P],
                                               qk[:, 2 * g + 1, begin:begin + width], start=True, stop=True)
                            mm.then_inc(score_mm, 1)
                        i, k = divmod(s - BATCH0 - 2, 2)
                        if k == 0 and 0 <= i < BATCHES:
                            multiply_batch(m, i)
                        if s == BATCH0 + 2 * BATCHES + 1:
                            multiply_pairs(m)
                        i, k = divmod(s - BATCH0, 2)
                        if k == 0 and 0 <= i < BATCHES:
                            if i < 3:
                                pe.wait_ge(mxs, m * (NG * T) + NG * T)
                            else:
                                pe.wait_ge(p_kept[(i - 3) % 2], kept_count(m, i - 3) + 1)
                            done = max(order.index((g, tile)) for g, tile, _ in batches[i]) + 1
                            pe.wait_ge(exps, m * (NG * T) + done)
                            for c, (g, tile, prev) in enumerate(batches[i]):
                                at, before = tile_at[g, tile]
                                at += P if before and not prev else 0
                                mm = pe.transpose(ring[(PAIRS + i) % 3][:, c * P:(c + 1) * P], sc[:, at:at + P],
                                                  r.ident[:, :])
                            mm.then_inc(p_turned, 1)
                    if n is not None:
                        q, third = divmod(s, 3)
                        j, half = divmod(q, 2)
                        if third == 0:
                            pe.wait_ge(w_low, n * B_UNITS + (j + 1))
                            if q > 1 or some(n):
                                pe.wait_ge(evac, n * B_HALVES + (q - 1))
                        mm = three_passes(pe, proj[half][:, :], w_hi[slot_of(j)], w_lo[slot_of(j)],
                                          r.h_hi, r.h_lo, slice(half * HALF, (half + 1) * HALF), third)
                        if third == 2:
                            mm.then_inc(proj_mm, 1)
                        q, k = divmod(s - 4, 3)
                        if k == 0 and 0 <= q < 12:
                            pe.wait_ge(evac, n * B_HALVES + (q + 1))
                            if q:
                                pe.wait_ge(rss, n * 12 + q)
                            elif some(n):
                                pe.wait_ge(v_kept, n * 6)
                            pe.matmul(side[:, :], r.ones[:, :], sg[:, q % 2], start=True, stop=True).then_inc(nsum, 1)
                        if s in V_TURNS:
                            c = V_TURNS.index(s)
                            g = c // 2
                            pe.wait_ge(evac, n * B_HALVES + (12 + 2 * g + 2))
                            if c:
                                pe.wait_ge(v_kept, n * 6 + c)
                            else:
                                pe.wait_ge(rss, n * 12 + 12)
                            for t in range(TH):
                                tile = (c % 2) * TH + t
                                if g == 0:
                                    tokens = slice(tile * P, (tile + 1) * P)
                                elif g == 1:
                                    b, res = divmod(tile, TH)
                                    tokens = slice(b * HALF + res, (b + 1) * HALF, TH)
                                else:
                                    tokens = slice(tile, S, T)
                                mm = pe.transpose(side[:, t * P:(t + 1) * P], v_raw[:, tokens], r.ident[:, :])
                            mm.then_inc(v_turned, 1)

            heads(pe, body)

        @block.vector
        def _(dve):
            for s_, c in ((qkn, 2), (v_turned, 2), (ogs, 2), (pv, 1), (nzr, 1), (lden, 1), (p_kept[0], 1),
                          (p_kept[1], 1), (o_stored, 16)):
                dve.sem_inc(s_, c)

            def split_low(n, j):
                dve.wait_ge(w_high, n * B_UNITS + (j + 1))
                dve.tensor_tensor(w_lo[slot_of(j)][:, :, :], raw[:, slot_of(j)], w_hi[slot_of(j)][:, :, :].bitcast(F32),
                                  ALU.subtract).then_inc(w_low, 1)

            split_low(0, 0)

            def body(m, n):
                last = isinstance(n, int) and n == H - 1
                for s in range(B_DELAYED):
                    if m is not None:
                        if s < PAIRS:
                            if s == 0:
                                dve.wait_ge(pv, m * (BATCHES + 1) + 1)
                                if some(m):
                                    dve.wait_ge(mmax, m * 2)
                            dve.wait_ge(score_mm, m * PAIRS + (s + 1))
                            dve.sem_inc(carrier, 1)
                            for c in range(2):
                                g, tile, at, first, width, before = score_tiles[2 * s + c]
                                mask = r.pair_mask[:, :] if g == 2 else r.band_mask[:, 2 * P - width:2 * P]
                                dve.tensor_tensor_reduce(sc[:, at:at + width], ring[s % 3][:, c * 2 * P:c * 2 * P + width],
                                                         mask, 1.0, -BIG, ALU.add, ALU.max,
                                                         mx[:, g, tile:tile + 1]).then_inc(mxs, 1)
                        if s == 17:
                            dve.wait_ge(mx_in, m * 32 + 32)
                            dve.wait_ge(mxs, m * (NG * T) + NG * T)
                            dve.tensor_tensor(mo[:, 0, :], mo[:, 0, :], mo[:, 1, :], ALU.max).then_inc(mmax, 1)
                            dve.wait_ge(mmax, m * 2 + 1)
                            dve.tensor_tensor(mo[:, 0, :], mo[:, 0, :], mx[:, 2, :], ALU.max).then_inc(mmax, 1)
                            dve.wait_ge(mmax, m * 2 + 2)
                            if some(m):
                                dve.wait_ge(exps, m * (NG * T))
                            dve.tensor_scalar(nb[:, 2, :], mo[:, 0, :], -SCORE, None, ALU.mult).then_inc(nbs, 1)
                        i, k = divmod(s - BATCH0 - 1, 2)
                        if k == 0 and 0 <= i < BATCHES and i % 2:
                            keep_batch(dve, m, i)
                        if s in (BATCH0 + 12, BATCH0 + 22):
                            half = (s - BATCH0 - 12) // 10
                            cols = slice(half * HALF, (half + 1) * HALF)
                            dve.wait_ge(half_mm, m * 2 + (half + 1))
                            dve.wait_ge(ogs, m * 2 + (half + 2))
                            dve.tensor_tensor(fin[:, 1], num[:, :], z[:, cols], ALU.mult).then_inc(nzr, 1)
                            dve.wait_ge(lden, m * 2 + (half + 1 + 1))
                            dve.wait_ge(zln, m * 2 + 2)
                            dve.tensor_tensor(fin[:, 0], fin[:, 0], zl[:, cols], ALU.add).then_inc(larg, 1)
                            dve.wait_ge(lexp, m * 2 + (half + 1))
                            dve.wait_ge(nzr, m * 2 + (half + 1 + 1))
                            dve.wait_ge(o_stored, m * 32 + (16 * half + 16))
                            dve.tensor_tensor(og[:, :], fin[:, 1], fin[:, 0], ALU.mult).then_inc(ogs, 1)
                    if n is not None:
                        if s < B_SLOTS and s % 6 == 3:
                            j = s // 6 + 1
                            if j < B_UNITS:
                                split_low(n, j)
                            elif not last:
                                split_low(n + 1, 0)
                        q, k = divmod(s - 4, 3)
                        if k == 0 and 0 <= q < 12:
                            half = q % 2
                            cols = slice(half * HALF, (half + 1) * HALF)
                            dve.wait_ge(rope, n * 12 + (q + 1))
                            if q:
                                dve.wait_ge(ropes, n * 48 + 4 * q)
                            elif some(n):
                                dve.wait_ge(ropes, n * 48)
                            dve.sem_inc(carrier, 1)
                            x = acc[0:ROPE, half]
                            dve.stream_shuffle(swap[:, :], x, [(i + HR) % ROPE for i in range(ROPE)]).then_inc(ropes, 1)
                            dve.wait_ge(ropes, n * 48 + (4 * q + 1))
                            dve.tensor_tensor(swap[:, :], swap[:, :], r.sin[:, cols], ALU.mult).then_inc(ropes, 1)
                            dve.tensor_tensor(x, x, r.cos[:, cols], ALU.mult).then_inc(ropes, 1)
                            dve.wait_ge(ropes, n * 48 + (4 * q + 3))
                            dve.tensor_tensor(x, x, swap[:, :], ALU.add).then_inc(ropes, 1)
                        q, k = divmod(s - 6, 3)
                        if k == 0 and 0 <= q < 12:
                            half, j = q % 2, q // 2
                            g = j // 2
                            dve.wait_ge(rs, n * 12 + (q + 1))
                            dve.wait_ge(ropes, n * 48 + (4 * q + 4))
                            if m is not None:
                                dve.wait_ge(score_mm, m * PAIRS + 4 * (g + 1))
                            a, b_ = acc[:, half], sg[:, half]
                            if g == 0:
                                out = qk[:, j, half * HALF:(half + 1) * HALF]
                            elif g == 1:
                                out = qk[:, j, :].rearrange("p (r i) -> p i r", r=TH)[:, half * P:(half + 1) * P, :]
                                a, b_ = (t.rearrange("p (i r) -> p i r", r=TH) for t in (a, b_))
                            else:
                                out = qk[:, j, :].rearrange("p (r i) -> p i r", r=T)[:, half * 64:(half + 1) * 64, :]
                                a, b_ = (t.rearrange("p (i r) -> p i r", r=T) for t in (a, b_))
                            dve.tensor_tensor(out, a, b_, ALU.mult).then_inc(qkn, 1)
                        q, k = divmod(s - 4, 3)
                        if k == 0 and B_HALVES - 2 <= q < B_HALVES:
                            half = q % 2
                            cols = slice(half * HALF, (half + 1) * HALF)
                            dve.wait_ge(evac, n * B_HALVES + (q + 1))
                            if m is not None:
                                dve.wait_ge(larg, m * 2 + 2)
                            dve.tensor_scalar(zl[:, cols], z[:, cols], -1.0, ARG_MAX, ALU.mult,
                                              ALU.min).then_inc(zarg, 1)

            heads(dve, body)


def allocate(nc, ctx):
    m = Mem(nc, ctx, "g")
    g = type("Resident", (), {})()
    g.h_hi = m.sb("h_hi", [P, KD, S], F32R)
    g.h_lo = m.sb("h_lo", [P, KD, S], F32R)
    g.ones = m.sb("ones", [P, P])
    g.ident = m.sb("ident", [P, P])
    g.tri = m.sb("tri", [P, P])
    g.decay_mask = m.sb("decay_mask", [P, P])
    g.level_mask = m.sb("level_mask", [P, LEVELS, P])
    g.gains = m.sb("gains", [P, 24])
    g.conv = m.sb("conv", [P, CONV, CT])
    g.head_bc = m.sb("head_bc", [P, 2 * H])
    return g


def program(nc, x, positions, norm_g, a_w_in, a_conv_w, a_log, a_dt_bias, a_norm_g, a_w_out,
            b_w_in, b_q_norm_g, b_k_norm_g, b_w_out, out):
    a_out = nc.dram_tensor("a_out", [A_VW, S], F32, kind="Internal").ap()
    x1 = nc.dram_tensor("x1", [S, D], F32, kind="Internal").ap()
    b_out = nc.dram_tensor("b_out", [D, S], F32, kind="Internal").ap()
    with ExitStack() as ctx:
        g = allocate(nc, ctx)
        constants(nc, g, norm_g, a_norm_g, b_q_norm_g, b_k_norm_g, a_conv_w, a_log, a_dt_bias)
        norm_and_turn(nc, "n0", g, x[0], 0)
        delta_heads(nc, g, a_w_in[0], a_out)
        out_projection(nc, "p0", a_out, a_w_out[0], x[0], x1, A_VW // P)
        norm_and_turn(nc, "n1", g, x1, 1)
        attention_heads(nc, g, b_w_in[0], positions, b_out)
        out_projection(nc, "p1", b_out, b_w_out[0], x1, out[0], D // P)


_INS = ["x", "positions", "norm_g", "a_w_in", "a_conv_w", "a_log", "a_dt_bias", "a_norm_g", "a_w_out",
        "b_w_in", "b_q_norm_g", "b_k_norm_g", "b_w_out"]


def kernel(**inputs):
    import numpy as _np
    import concourse.bacc as _bacc
    from concourse import mybir as _mybir
    from concourse.bass_utils import run_bass_kernel_spmd as _run

    nc = _bacc.Bacc("TRN2", target_bir_lowering=False, num_devices=1)
    arrays, args = {}, []
    for name in _INS:
        a = _np.ascontiguousarray(inputs[name])
        arrays[f"in_{name}_dram"] = a
        args.append(nc.dram_tensor(f"in_{name}_dram", a.shape, _mybir.dt.from_np(a.dtype), kind="ExternalInput").ap())
    out = nc.dram_tensor("out_0_dram", (1, S, D), _mybir.dt.float32, kind="ExternalOutput").ap()
    program(nc, *args, out)
    r = _run(nc, [arrays], core_ids=[0])
    return r.results[0]["out_0_dram"]
```

```python
from contextlib import ExitStack

import numpy as np

import concourse.bass as bass
from concourse import mybir

F32 = mybir.dt.float32
F32R = mybir.dt.float32r
I32 = mybir.dt.int32
ALU = mybir.AluOpType
ACT = mybir.ActivationFunctionType

P = 128
S = 1024
D = 1024
T = S // P
KD = D // P
HALF = 512
TH = HALF // P
H = D // P
DK = 128
DV = 256
VT = DV // P
A_QK = H * DK
A_VW = H * DV
CONV = 4
CT = (2 * A_QK + A_VW) // P
EPS = 1e-6
EXP_LN = "natural_log_exp_and_others"
BIG = 1e30
ARG_MAX = 44.0
BLK = 16
NB = P // BLK
LEVELS = 3
BLOCK_STEP = BLK * (P + 1)
TILE_STEP = NB * BLOCK_STEP

NG = 3
ROPE = 32
HR = ROPE // 2
THETA = 500000.0


def spread(ap, axis, n):
    v = ap.unsqueeze(axis)
    shape = list(v.shape)
    shape[axis] = n
    return v.broadcast_to(shape)


class Mem:

    def __init__(self, nc, ctx, tag):
        self.nc, self.ctx, self.tag = nc, ctx, tag

    def sb(self, name, shape, dt=F32):
        return self.ctx.enter_context(self.nc.sbuf_tensor(f"{self.tag}_{name}", shape, dt))

    def ps(self, name, shape, dt=F32):
        return self.ctx.enter_context(self.nc.psum_tensor(f"{self.tag}_{name}", shape, dt))

    def sem(self, name):
        return self.ctx.enter_context(self.nc.semaphore(f"{self.tag}_{name}"))


def constants(nc, g, norm_g, a_norm_g, b_q_norm_g, b_k_norm_g, a_conv_w, a_log, a_dt_bias):
    with ExitStack() as ctx:
        m = Mem(nc, ctx, "c")
        rows = m.sb("rows", [24, P])
        conv_rows = m.sb("conv_rows", [P, P])
        head_row = m.sb("head_row", [1, 2 * H])
        freq_row = m.sb("freq_row", [1, 2 * ROPE])
        sign_row = m.sb("sign_row", [1, P])
        ps = m.ps("ps", [P, 512])
        freq = (np.float32(THETA) ** (-np.arange(0, ROPE, 2, dtype=np.float32) / np.float32(ROPE))).astype(np.float32)
        rows_made = m.sem("rows_made")
        zero = m.sem("zero")
        made = m.sem("made")
        landed = m.sem("landed")
        turned = m.sem("turned")
        kept = m.sem("kept")
        block = ctx.enter_context(nc.Block())

        @block.sync
        def _(sp):
            sp.dma_start(rows[0:16, :], norm_g.rearrange("l (k c) -> (l k) c", c=P)).then_inc(landed, 16)
            sp.dma_start(rows[16:18, :], a_norm_g.rearrange("l (k c) -> (l k) c", c=P)).then_inc(landed, 16)
            sp.dma_start(rows[18:21, :], b_q_norm_g.rearrange("l g c -> (l g) c")).then_inc(landed, 16)
            sp.dma_start(rows[21:24, :], b_k_norm_g.rearrange("l g c -> (l g) c")).then_inc(landed, 16)
            sp.dma_start(conv_rows[:, :], a_conv_w.rearrange("l j (c n) -> (l j c) n", n=P)).then_inc(landed, 16)
            sp.dma_start(head_row[:, 0:H], a_log).then_inc(landed, 16)
            sp.dma_start(head_row[:, H:2 * H], a_dt_bias).then_inc(landed, 16)

        @block.gpsimd
        def _(pool):
            def ones(ap):
                pool.memset(ap, 1.0).then_inc(zero, 1)

            cuts = []

            def keep(ap, pattern, base, mult, op, fill):
                if cuts:
                    pool.wait_ge(made, len(cuts))
                cuts.append(ap)
                pool.affine_select(out=ap, in_=ap, compare_op=op, fill=fill, base=base,
                                   pattern=pattern, channel_multiplier=mult).then_inc(made, 1)

            ones(g.ones[:, :])
            pool.memset(g.ident[:, :], 0.0).then_inc(zero, 1)
            ones(g.tri[:, :])
            pool.memset(g.decay_mask[:, :], 0.0).then_inc(zero, 1)
            ones(g.level_mask[:, :, :])
            pool.wait_ge(zero, 5)
            keep(g.ident[:, :], [[-1, P]], 0, 1, ALU.not_equal, 1.0)
            keep(g.tri[:, :], [[1, P]], 0, -1, ALU.is_ge, 0.0)
            keep(g.decay_mask[:, :], [[1, P]], 0, -1, ALU.is_ge, -BIG)
            for level in range(LEVELS):
                size = BLK << level
                pairs = P // (2 * size)
                cell = g.level_mask[:, level, :].rearrange("p (c e r) -> p c e r", e=2, r=size)
                for across, within, base, mult in ((0, 1, -1, 0), (-2 * size, 0, 0, 1), (2 * size, 0, size - 1, -1)):
                    if pairs > 1:
                        keep(cell, [[across, pairs], [within, 2], [0, size]], base, mult, ALU.is_ge, 0.0)
                    else:
                        keep(cell[:, 0], [[within, 2], [0, size]], base, mult, ALU.is_ge, 0.0)
            pool.memset(g.band_mask[:, :], 0.0).then_inc(zero, 1)
            pool.wait_ge(zero, 6)
            keep(g.band_mask[:, 0:P], [[1, P]], 0, -1, ALU.is_ge, -BIG)
            keep(g.band_mask[:, P:], [[-1, P]], 0, 1, ALU.is_ge, -BIG)
            pool.wait_ge(kept, 5)
            keep(g.pair_mask[:, :], [[-1, P]], 0, 1, ALU.is_ge, -BIG)
            pool.wait_ge(made, len(cuts))

        @block.tensor
        def _(pe):
            pe.wait_ge(rows_made, HR + 4)
            pe.wait_ge(zero, 5)
            pe.matmul(ps[0:ROPE, 288:289], freq_row[:, 0:ROPE], g.ones[0:1, 0:1], start=True, stop=True)
            pe.matmul(ps[0:ROPE, 289:290], freq_row[:, ROPE:], g.ones[0:1, 0:1], start=True, stop=True)
            pe.matmul(ps[:, 384:512], sign_row[:, :], sign_row[:, :], start=True, stop=True)
            pe.wait_ge(landed, 7 * 16)
            pe.wait_ge(made, 1)
            pe.transpose(ps[:, 0:24], rows[:, :], g.ident[0:24, 0:24])
            pe.transpose(ps[:, 128:256], conv_rows[:, :], g.ident[:, :])
            pe.matmul(ps[:, 256:256 + 2 * H], g.ones[0:1, :], head_row[:, :], start=True, stop=True).then_inc(turned, 1)

        @block.vector
        def _(dve):
            for i in range(HR):
                dve.memset(freq_row[:, i:i + HR + 1:HR], float(freq[i])).then_inc(rows_made, 1)
            dve.memset(freq_row[:, ROPE:ROPE + HR], -1.0).then_inc(rows_made, 1)
            dve.memset(freq_row[:, ROPE + HR:], 1.0).then_inc(rows_made, 1)
            dve.memset(sign_row[:, 0::2], 1.0).then_inc(rows_made, 1)
            dve.memset(sign_row[:, 1::2], -1.0).then_inc(rows_made, 1)
            dve.memset(g.ones_r[:, :].bitcast(F32), 1.0).then_inc(rows_made, 1)
            dve.wait_ge(turned, 1)
            dve.tensor_copy(g.gains[:, :], ps[:, 0:24]).then_inc(kept, 1)
            dve.tensor_copy(g.conv[:, :, :], ps[:, 128:256].rearrange("p (j c) -> p j c", j=CONV)).then_inc(kept, 1)
            dve.tensor_copy(g.head_bc[:, :], ps[:, 256:256 + 2 * H]).then_inc(kept, 1)
            dve.tensor_copy(g.freq[:, :], ps[0:ROPE, 288:290]).then_inc(kept, 1)
            dve.tensor_scalar(g.pair_mask[:, :], ps[:, 384:512], -1.0, BIG / 2, ALU.add, ALU.mult).then_inc(kept, 1)


class WeightSlots:

    def __init__(self, nc, ctx, tag, w, first, split_both):
        m = Mem(nc, ctx, tag)
        self.raw = m.sb("raw", [P, 2, KD, P])
        self.hi = [m.sb(f"w_hi{i}", [P, KD, P], F32R) for i in range(2)]
        self.lo = [m.sb(f"w_lo{i}", [P, KD, P], F32R) for i in range(2)]
        self.landed = [m.sem("w_landed0"), m.sem("w_landed1")]
        if first[0][1] < P:
            self.cleared = m.sem("cleared")
        self.high, self.low = m.sem("w_high"), m.sem("w_low")
        self.w, self.first, self.split_both = w, first, split_both

    def load(self, sp):
        for slot, (at, width) in enumerate(self.first):
            if width < P:
                sp.wait_ge(self.cleared, 1)
            sp.dma_start(self.raw[:, slot, :, 0:width], self.w[:, at:at + width].rearrange("(k p) c -> p k c", p=P)
                         ).then_inc(self.landed[slot], 16)

    def clear(self, dve):
        if self.first[0][1] < P:
            dve.memset(self.raw[:, 0], 0.0).then_inc(self.cleared, 1)

    def split_high(self, act):
        for slot in range(1 + self.split_both):
            act.wait_ge(self.landed[slot], 16)
            act.activation(self.hi[slot][:, :, :], self.raw[:, slot], ACT.Copy).then_inc(self.high, 1)

    def split_low(self, dve):
        for slot in range(1 + self.split_both):
            dve.wait_ge(self.high, slot + 1)
            dve.tensor_tensor(self.lo[slot][:, :, :], self.raw[:, slot], self.hi[slot][:, :, :].bitcast(F32),
                              ALU.subtract).then_inc(self.low, 1)


def norm_and_turn(nc, tag, g, src, layer, weights):
    RING = 4
    with ExitStack() as ctx:
        m = Mem(nc, ctx, tag)
        x = m.sb("x", [P, T, D])
        sq = m.sb("sq", [P, D])
        stat = m.sb("stat", [P, T, 3])
        diag = m.sb("diag", [P, RING, P])
        hf = m.sb("hf", [P, RING, KD, P])
        turned_ps = m.ps("turned_ps", [P, RING, KD, P])
        loads = ((0, 1), (1, 2), (2, 5), (5, T))
        landed = [m.sem(f"landed{i}") for i in range(len(loads))]
        load_of = [i for i, (a, b) in enumerate(loads) for _ in range(a, b)]
        stats = m.sem("stats")
        scales = m.sem("scales")
        turned = m.sem("turned")
        gained = m.sem("gained")
        high = m.sem("high")
        low = m.sem("low")
        block = ctx.enter_context(nc.Block())
        gain = g.gains[:, layer * KD:(layer + 1) * KD]

        def tokens(t):
            return slice(t * P, (t + 1) * P)

        @block.sync
        def _(sp):
            for i, (a, b) in enumerate(loads):
                sp.dma_start(x[:, a:b, :], src[a * P:b * P, :].rearrange("(t p) n -> p t n", p=P)
                             ).then_inc(landed[i], 16)
            weights.load(sp)

        @block.scalar
        def _(act):
            act.preload_act_table_set(EXP_LN)
            for t in range(T + 2):
                if t < T:
                    act.wait_ge(landed[load_of[t]], 16)
                    act.activation(sq[:, :], x[:, t, :], ACT.Square, accum_out=stat[:, t, 0:1]).then_inc(stats, 1)
                    act.wait_ge(stats, 3 * t + 1)
                    act.activation(stat[:, t, 1:2], stat[:, t, 0:1], ACT.Ln, scale=1.0 / D, bias=EPS).then_inc(stats, 1)
                    act.wait_ge(stats, 3 * t + 2)
                    act.activation(stat[:, t, 2:3], stat[:, t, 1:2], ACT.Exp, scale=-0.5).then_inc(stats, 1)
                if t == T:
                    weights.split_high(act)
                if t >= 2:
                    act.wait_ge(gained, t - 1)
                    act.activation(g.h_hi[:, :, tokens(t - 2)], hf[:, (t - 2) % RING], ACT.Copy).then_inc(high, 1)

        @block.tensor
        def _(pe):
            for t in range(T):
                pe.wait_ge(landed[load_of[t]], 16)
                pe.wait_ge(scales, t + 1)
                if t >= RING:
                    pe.wait_ge(gained, t - RING + 1)
                for k in range(KD):
                    last = pe.matmul(turned_ps[:, t % RING, k, :], x[:, t, k * P:(k + 1) * P], diag[:, t % RING, :],
                                     start=True, stop=True)
                last.then_inc(turned, 1)

        @block.vector
        def _(dve):
            weights.clear(dve)
            for t in range(T + 2):
                if t < T:
                    dve.wait_ge(stats, 3 * t + 3)
                    if t >= RING:
                        dve.wait_ge(turned, t - RING + 1)
                    dve.tensor_scalar(diag[:, t % RING, :], g.ident[:, :], stat[:, t, 2:3], None,
                                      ALU.mult).then_inc(scales, 1)
                if 1 <= t <= T:
                    dve.wait_ge(turned, t)
                    if t > RING:
                        dve.wait_ge(low, t - RING)
                    dve.tensor_tensor(hf[:, (t - 1) % RING], turned_ps[:, (t - 1) % RING], spread(gain, 2, P),
                                      ALU.mult).then_inc(gained, 1)
                if t == T + 1:
                    weights.split_low(dve)
                if t >= 2:
                    dve.wait_ge(high, t - 1)
                    dve.tensor_tensor(g.h_lo[:, :, tokens(t - 2)], hf[:, (t - 2) % RING],
                                      g.h_hi[:, :, tokens(t - 2)].bitcast(F32), ALU.subtract).then_inc(low, 1)


SLOTS = 36
UNITS = 6
HALVES = 2 * UNITS
LEVEL0 = 1
DECAYS = (12, 15)
CHAIN0 = 7
K_TURNS = (22, 34)
GRAM0 = 19
BLOCKS_OUT = GRAM0 + T + 1
DELAYED = SLOTS + 6


def three_passes(pe, out, w_hi, w_lo, a_hi, a_lo, ks, third):
    last = None
    for n in range(8 * third, 8 * third + 8):
        k, c = n // 3, n % 3
        w = (w_hi, w_hi, w_lo)[c]
        a = (a_hi, a_lo, a_hi)[c]
        last = pe.matmul(out, w[:, k, :], a[:, k, ks], start=(n == 0), stop=(n == 23))
    return last


def delta_heads(nc, g, weights, o_turned):
    with ExitStack() as ctx:
        m_ = Mem(nc, ctx, "a")
        raw, w_hi, w_lo = weights.raw, weights.hi, weights.lo
        x_raw = m_.sb("x_raw", [P, CONV - 1 + S])
        acc = m_.sb("acc", [P, 2, HALF])
        sg = m_.sb("sg", [P, 2, HALF])
        kq = m_.sb("kq", [P, 2, T, 2, P])
        v = m_.sb("v", [P, 2, T, DV])
        z = m_.sb("z", [P, 2, VT, S])
        attn = m_.sb("attn", [P, 2, T, P])
        kd = m_.sb("kd", [P, T, P])
        u = m_.sb("u", [P, T, P])
        zx = m_.sb("zx", [P, T, 2, P])
        zf = m_.sb("zf", [P, T, P])
        cols = m_.sb("cols", [P, 7, T, H])
        hc = m_.sb("hc", [P, 2, 7, T])
        hw = m_.sb("hw", [P, 2, CONV, 4])
        bd = m_.sb("bd", [NB * T, BLK, BLK])
        bx = m_.sb("bx", [NB * T, BLK, BLK])
        bt = m_.sb("bt", [NB * T, (BLK // 2) ** 2])
        dec = m_.sb("dec", [P, T, P])
        um = m_.sb("um", [P, 2, LEVELS, P])
        bc = m_.sb("bc", [P, 2, P])
        zx1 = m_.sb("zx1", [P, 2, 2, P])
        state = m_.sb("state", [P, 2, DV])
        r = m_.sb("r", [P, DV])
        vn = m_.sb("vn", [P, DV])
        o1 = m_.sb("o1", [P, 2, DV])
        o = m_.sb("o", [P, 2, DV])
        ostat = m_.sb("ostat", [P, 2, 3])
        og = m_.sb("og", [P, VT, P])
        ba = acc[0:2 * H].rearrange("p b i -> p (b i)")
        tmp = sg[:, 0, 0:3 * T * H].rearrange("p (a t h) -> p a t h", a=3, t=T)
        neg_a = m_.sb("neg_a", [P, H])
        C_CUM, C_EXP, C_NEXP, C_BETA, C_TAIL, C_LAST, C_LOG = range(7)

        u_dram = nc.dram_tensor("u_tiles", [T * TILE_STEP], F32, kind="Internal").ap()
        inv_dram = nc.dram_tensor("inverse_tiles", [2, T * TILE_STEP], F32, kind="Internal").ap()

        def as_tiles(flat):
            return (flat.rearrange("(t x) -> t x", x=TILE_STEP)[:, 0:P * P]
                    .rearrange("t (j i) -> j t i", j=P))

        def as_blocks(flat):
            return (flat.rearrange("(p x) -> p x", x=BLOCK_STEP)[:, 0:BLK * P]
                    .rearrange("p (j i) -> p j i", i=P)[:, :, 0:BLK])

        proj = [m_.ps(f"proj{i}", [P, HALF]) for i in range(2)]
        step = m_.ps("step", [P, 2, DV])
        new = m_.ps("new", [P, DV])
        first = m_.ps("first", [P, 2, P])
        lev = m_.ps("lev", [P, 2, 2, P])
        turn = m_.ps("turn", [P, HALF])
        gram = m_.ps("gram", [P, HALF])

        sem = m_.sem
        w_landed, w_high, w_low = weights.landed, weights.high, weights.low
        proj_mm, evac = sem("proj_mm"), sem("evac")
        arg, sig, act_out = sem("arg"), sem("sig"), sem("act_out")
        sigs = sem("sigs")
        convs, taps = sem("convs"), sem("taps")
        sq, nsum, rs, rss, kqn = sem("sq"), sem("nsum"), sem("rs"), sem("rss"), sem("kqn")
        v_turned, v_kept = sem("v_turned"), sem("v_kept")
        k_turned, k_kept = sem("k_turned"), sem("k_kept")
        k_tail = sem("k_tail")
        row_mm = sem("row_mm")
        gram_mm, darg, dexp, ut = sem("gram_mm"), sem("darg"), sem("dexp"), sem("ut")
        blocks_out, blocks_in, blocks_inv = sem("blocks_out"), sem("blocks_in"), sem("blocks_inv")
        inv_out, inv_zero = sem("inv_out"), sem("inv_zero")
        back = [sem("back_first"), sem("back_rest")]
        bstep = sem("bstep")
        zx_zero = sem("zx_zero")
        um_s, first_mm, first_c, lv_mm, lv_s = (sem(x) for x in ("um", "first_mm", "first_c", "lv_mm", "lv_s"))
        ks_mm, r_s, xr_mm, vn_s = sem("ks_mm"), sem("r_s"), sem("xr_mm"), sem("vn_s")
        osu_mm, o1_s, st_s, o_s = sem("osu_mm"), sem("o1_s"), sem("st_s"), sem("o_s")
        ostats, on_s, o_mm, og_s = sem("ostats"), sem("on_s"), sem("o_mm"), sem("og_s")
        o_stored = sem("o_stored")
        hc_s = sem("hc_s")
        setup = sem("setup")
        cols_s = sem("cols_s")
        totals = sem("totals")
        carrier = sem("carrier")
        block = ctx.enter_context(nc.Block())

        def col_of(n, j):
            if j == 0:
                return n * P + A_QK
            if j == 1:
                return n * P
            if j < 4:
                return n * DV + (2 * A_QK + (j - 2) * P)
            return n * DV + (2 * A_QK + A_VW + (j - 4) * P)

        def slot_of(j):
            return (1 + j) % 2

        def landed_of(n, j):
            return 16 * (n * (UNITS // 2) + (1 + j) // 2 + 1)

        def turn_order(mix, nxt):
            uses = []
            for s in range(SLOTS):
                if mix and (s - CHAIN0 - 6) % 3 == 0 and 0 <= (s - CHAIN0 - 6) // 3 < T:
                    uses.append(("o", (s - CHAIN0 - 6) // 3))
                if nxt and s in (8, 11, 14, 17):
                    uses.append(("sum", (s - 8) // 3))
                if nxt and s in K_TURNS:
                    uses.append(("k", K_TURNS.index(s)))
                if nxt and s in (20, 23, 26, 29):
                    uses.append(("v", (s - 20) // 3))
            return uses

        def heads(eng, body):
            body(None, 0, 0)
            with eng.Fori(0, H // 2 - 1) as i:
                body(i * 2, i * 2 + 1, 1)
                body(i * 2 + 1, i * 2 + 2, 0)
            body(H - 2, H - 1, 1)
            body(H - 1, None, 0)

        @block.sync
        def _(sp):
            def load(n, j):
                sp.wait_ge(w_low, n * UNITS + j)
                sp.sem_inc(carrier, 1)
                sp.dma_start(raw[:, slot_of(j)], weights.w[:, bass.ds(col_of(n, j), P)]
                             .rearrange("(k p) c -> p k c", p=P)).then_inc(w_landed[slot_of(j)], 16)

            sp.wait_ge(zx_zero, 1)
            for c in range(2):
                sp.dma_start(as_tiles(inv_dram[c]), zx[:, :, c, :]).then_inc(inv_zero, 16)
            sp.wait_ge(inv_zero, 32)

            def body(m, n, p):
                for s in range(DELAYED):
                    if m is not None and s == 0:
                        sp.wait_ge(blocks_inv, m * 2 + 2)
                        sp.wait_ge(lv_s, m * (LEVELS * T // 2) + 1)
                        sp.dma_start(as_blocks(inv_dram[0]), bd[:, :, :]).then_inc(inv_out, 16)
                        sp.dma_start(as_blocks(inv_dram[1]), bx[:, :, :]).then_inc(inv_out, 16)
                        sp.wait_ge(inv_out, m * 32 + 32)
                        for part, tiles in enumerate((slice(0, 2), slice(2, T))):
                            for c in range(2):
                                sp.dma_start(zx[:, tiles, c, :], as_tiles(inv_dram[c])[:, tiles]
                                             ).then_inc(back[part], 16)
                    if n is not None and s < SLOTS and s % 6 == 3:
                        j = s // 6 + 1
                        if j < UNITS:
                            load(n, j)
                        elif not (isinstance(n, int) and n == H - 1):
                            load(n + 1, 0)
                    if n is not None and s == BLOCKS_OUT:
                        sp.wait_ge(ut, n * (T // 2) + T // 2)
                        sp.dma_start(as_tiles(u_dram), u[:, :, :]).then_inc(blocks_out, 16)
                        if not (isinstance(n, int) and n == 0):
                            sp.wait_ge(inv_out, n * 32)
                        sp.wait_ge(blocks_out, n * 16 + 16)
                        sp.dma_start(bd[:, :, :], as_blocks(u_dram)).then_inc(blocks_in, 16)
                    if m is not None and (s - CHAIN0 - 8) % 3 == 0 and 0 <= (s - CHAIN0 - 8) // 3 < T:
                        t = (s - CHAIN0 - 8) // 3
                        sp.wait_ge(og_s, m * T + (t + 1 + T))
                        dst = o_turned[bass.ds(m * DV, DV), t * P:(t + 1) * P].rearrange("(c p) n -> p c n", p=P)
                        sp.dma_start(dst, og[:, :, :]).then_inc(o_stored, 16)

            heads(sp, body)
            sp.wait_ge(o_stored, 16 * (1 + H * T))

        @block.gpsimd
        def _(pool):
            pool.memset(zx[:, :, :, :], 0.0).then_inc(zx_zero, 1)
            pool.wait_ge(cols_s, 1)

            def body(m, n, p):
                if n is not None:
                    columns_and_taps(n, p)
                if m is not None:
                    for b in range(T // 2):
                        pool.wait_ge(first_mm, m * (LEVELS * T // 2) + (LEVELS * b + 1))
                        pool.wait_ge(ut, m * (T // 2) + (b + 1))
                        pool.tensor_tensor(um[:, :, :, :], spread(u[:, 2 * b:2 * b + 2, :], 2, LEVELS),
                                           spread(g.level_mask[:, :, :], 1, 2), ALU.mult).then_inc(um_s, 1)
                if n is not None:
                    invert_blocks(n)

            def columns_and_taps(n, p):
                pool.wait_ge(og_s, n * T)
                pool.tensor_copy(hc[:, p], cols[:, :, :, bass.ds(n, 1)].rearrange("p a t o -> p a (t o)")
                                 ).then_inc(hc_s, 1)
                for c, tile in ((0, n + H), (1, n + 0), (2, n * 2 + 2 * H), (3, n * 2 + (2 * H + 1))):
                    pool.tensor_copy(hw[:, p, :, c:c + 1], g.conv[:, :, bass.ds(tile, 1)]).then_inc(hc_s, 1)

            def invert_blocks(n):
                if not (isinstance(n, int) and n == 0):
                    pool.wait_ge(inv_out, n * 32)
                pool.sem_inc(carrier, 1)
                pool.memset(bx[:, :, :], 0.0).then_inc(bstep, 1)
                pool.wait_ge(bstep, n * (2 * BLK) + 1)
                pool.sem_inc(carrier, 1)
                pool.tensor_copy(bx[:, :, :].rearrange("t j i -> t (j i)")[:, 0:BLK * BLK:BLK + 1],
                                 g.ones[0:NB * T, 0:BLK]).then_inc(bstep, 1)
                pool.wait_ge(blocks_in, n * 16 + 16)
                for j in range(BLK - 1):
                    pool.wait_ge(bstep, n * (2 * BLK) + (2 + 2 * j))
                    rows, width = BLK - 1 - j, j + 1
                    prod = bt[:, 0:rows * width].rearrange("t (i c) -> t i c", c=width)
                    pool.tensor_tensor(prod, spread(bd[:, j, j + 1:BLK], 2, width),
                                       spread(bx[:, j, 0:width], 1, rows), ALU.mult).then_inc(bstep, 1)
                    pool.wait_ge(bstep, n * (2 * BLK) + (3 + 2 * j))
                    pool.tensor_tensor(bx[:, j + 1:BLK, 0:width], bx[:, j + 1:BLK, 0:width], prod,
                                       ALU.subtract).then_inc(bstep if j < BLK - 2 else blocks_inv, 1)
                pool.wait_ge(blocks_inv, n * 2 + 1)
                pool.sem_inc(carrier, 1)
                pool.tensor_copy(bd[:, :, :], bx[:, :, :].rearrange("t i c -> t c i")).then_inc(blocks_inv, 1)
                pool.wait_ge(blocks_inv, n * 2 + 2)
                pool.sem_inc(bstep, 1)

            heads(pool, body)

        @block.scalar
        def _(act):
            def split_high(idx, slot, landed):
                act.wait_ge(w_landed[slot], landed)
                act.wait_ge(proj_mm, idx * 2 - 2)
                act.activation(w_hi[slot][:, :, :], raw[:, slot], ACT.Copy).then_inc(w_high, 1)

            act.preload_act_table_set(EXP_LN)
            for b in range(2):
                act.wait_ge(proj_mm, b + 1)
                act.activation(ba[:, b * HALF:(b + 1) * HALF], proj[b][0:2 * H, :], ACT.Copy).then_inc(evac, 1)
            act.wait_ge(setup, 3)
            act.activation(neg_a[:, :], g.head_bc[:, 0:H], ACT.Exp).then_inc(setup, 1)
            act.activation(tmp[:, 0], tmp[:, 0], ACT.Exp).then_inc(setup, 1)
            act.activation(tmp[:, 2], tmp[:, 1], ACT.Abs).then_inc(setup, 1)
            act.wait_ge(setup, 6)
            act.activation(tmp[:, 0], tmp[:, 0], ACT.Ln, bias=1.0).then_inc(setup, 1)
            act.activation(tmp[:, 2], tmp[:, 2], ACT.Exp, scale=-1.0).then_inc(setup, 1)
            act.wait_ge(setup, 8)
            act.activation(cols[:, C_BETA], tmp[:, 0], ACT.Exp, scale=-1.0).then_inc(setup, 1)
            act.activation(tmp[:, 2], tmp[:, 2], ACT.Ln, bias=1.0).then_inc(setup, 1)
            act.wait_ge(setup, 14)
            act.activation(cols[:, C_EXP], cols[:, C_CUM], ACT.Exp).then_inc(setup, 1)
            act.activation(cols[:, C_LAST], tmp[:, 0], ACT.Exp).then_inc(setup, 1)
            act.activation(cols[:, C_TAIL], tmp[:, 1], ACT.Exp).then_inc(setup, 1)

            def body(m, n, p):
                pm = 1 - p
                for s in range(DELAYED):
                    if m is not None:
                        b, k = divmod(s - LEVEL0 - 1, 6)
                        if 0 <= b < T // 2 and k % 2 == 0:
                            use = LEVELS * b + k // 2
                            act.wait_ge(first_mm, m * (LEVELS * T // 2) + (use + 1 + 1))
                            act.activation(bc[:, :, :], first[:, :, :], ACT.Copy).then_inc(first_c, 1)
                        t, k = divmod(s - CHAIN0, 3)
                        if 0 <= t < T and k == 0:
                            act.wait_ge(r_s, m * T + (t + 1))
                            act.wait_ge(o_s, m * T + (t - 1 + 2))
                            act.wait_ge(ostats, m * (3 * T) + (3 * (t - 2) + 1 + 6))
                            act.activation(o1[:, t % 2, :], step[:, 1], ACT.Copy,
                                           scale=hc[:, pm, C_EXP, t:t + 1]).then_inc(o1_s, 1)
                        if 0 <= t < T and k == 1:
                            act.wait_ge(xr_mm, m * T + (t + 1))
                            act.wait_ge(osu_mm, m * T + (t + 1))
                            act.activation(vn[:, :], new[:, :], ACT.Copy,
                                           scale=hc[:, pm, C_BETA, t:t + 1]).then_inc(vn_s, 1)
                        t, k = divmod(s - CHAIN0 - 4, 3)
                        if 0 <= t < T and k == 0:
                            act.wait_ge(o_s, m * T + (t + 1 + 2))
                            act.activation(o1[:, t % 2, :], o[:, t % 2, :], ACT.Square,
                                           accum_out=ostat[:, t % 2, 0:1]).then_inc(ostats, 1)
                            act.wait_ge(ostats, m * (3 * T) + (3 * t + 1 + 6))
                            act.activation(ostat[:, t % 2, 1:2], ostat[:, t % 2, 0:1], ACT.Ln,
                                           scale=1.0 / DV, bias=EPS).then_inc(ostats, 1)
                            act.wait_ge(ostats, m * (3 * T) + (3 * t + 2 + 6))
                            act.activation(ostat[:, t % 2, 2:3], ostat[:, t % 2, 1:2], ACT.Exp,
                                           scale=-0.5).then_inc(ostats, 1)
                            act.wait_ge(ostats, m * (3 * T) + (3 * t + 3 + 6))
                            act.activation(o[:, t % 2, :], o[:, t % 2, :], ACT.Copy,
                                           scale=ostat[:, t % 2, 2:3]).then_inc(on_s, 1)
                    if n is not None:
                        if s < SLOTS and s % 6 == 2:
                            j = s // 6 + 1
                            if j < UNITS:
                                split_high(n * UNITS + (1 + j), slot_of(j), landed_of(n, j))
                            elif not (isinstance(n, int) and n == H - 1):
                                split_high(n * UNITS + (1 + j), slot_of(0), landed_of(n + 1, 0))
                        q, k = divmod(s - 3, 3)
                        if 0 <= q < HALVES and k == 0:
                            half = q % 2
                            act.wait_ge(proj_mm, n * HALVES + (q + 3))
                            if q < 8:
                                act.wait_ge(convs, n * 8 + (q // 2 * 2 + 1))
                                act.activation(x_raw[:, CONV - 1 + half * HALF:CONV - 1 + (half + 1) * HALF],
                                               proj[half][:, :], ACT.Copy).then_inc(evac, 1)
                            else:
                                if q < 10:
                                    act.wait_ge(v_turned, n * 4 + (q - 5))
                                else:
                                    act.wait_ge(act_out, n * HALVES + (q - 1 + 2))
                                act.activation(acc[:, half], proj[half][:, :], ACT.Copy).then_inc(evac, 1)
                        q, k = divmod(s - 5, 3)
                        if 0 <= q < HALVES and k == 0:
                            act.wait_ge(arg, n * HALVES + (q + 1))
                            act.activation(sg[:, q % 2], sg[:, q % 2], ACT.Exp).then_inc(sigs, 1)
                            act.wait_ge(sigs, n * (2 * HALVES) + (2 * q + 1))
                            act.activation(sg[:, q % 2], sg[:, q % 2], ACT.Ln, bias=1.0).then_inc(sigs, 1)
                            act.wait_ge(sigs, n * (2 * HALVES) + (2 * q + 2))
                            act.activation(sg[:, q % 2], sg[:, q % 2], ACT.Exp, scale=-1.0).then_inc(sig, 1)
                        q, k = divmod(s - 7, 3)
                        if 0 <= q < 4 and k == 0:
                            act.wait_ge(act_out, n * HALVES + (q + 1 + 2))
                            act.activation(sg[:, q % 2], acc[:, q % 2], ACT.Square).then_inc(sq, 1)
                        q, k = divmod(s - 9, 3)
                        if 0 <= q < 4 and k == 0:
                            act.wait_ge(nsum, n * 4 + (q + 1))
                            act.activation(sg[:, q % 2], turn[:, :], ACT.Ln, bias=EPS).then_inc(rss, 1)
                            act.wait_ge(rss, n * 4 + (q + 1))
                            act.activation(sg[:, q % 2], sg[:, q % 2], ACT.Exp, scale=-0.5,
                                           bias=0.0 if q < 2 else -0.5 * float(np.log(DK))).then_inc(rs, 1)
                        if 4 <= q < 8 and k == 0:
                            act.wait_ge(v_turned, n * 4 + (q - 3))
                            c = q // 2 - 2
                            act.activation(v[:, p, (q % 2) * TH:(q % 2 + 1) * TH, c * P:(c + 1) * P],
                                           turn[:, :].rearrange("p (t c) -> p t c", t=TH),
                                           ACT.Copy).then_inc(v_kept, 1)
                        if s - 1 in DECAYS:
                            half = DECAYS.index(s - 1)
                            tiles = dec[:, half * TH:(half + 1) * TH, :]
                            act.wait_ge(darg, n * T + (half + 1) * TH)
                            act.activation(tiles, tiles, ACT.Exp).then_inc(dexp, 1)

            heads(act, body)

        @block.tensor
        def _(pe):
            pe.wait_ge(w_low, 1)
            for b in range(2):
                for third in range(3):
                    last = three_passes(pe, proj[b][:, :], w_hi[0], w_lo[0], g.h_hi, g.h_lo,
                                        slice(b * HALF, (b + 1) * HALF), third)
                last.then_inc(proj_mm, 1)
            pe.wait_ge(evac, 2)
            for t in range(T):
                last = pe.transpose(turn[:, t * 2 * H:(t + 1) * 2 * H], ba[:, t * P:(t + 1) * P],
                                    g.ident[0:2 * H, 0:2 * H])
            last.then_inc(setup, 1)
            pe.wait_ge(setup, 12)
            log = cols[:, C_LOG].rearrange("p t h -> p (t h)")
            pe.matmul(turn[:, 256:256 + T * H], g.tri[:, :], log, start=True, stop=True)
            pe.matmul(turn[:, 384:384 + T * H], g.ones[:, :], log, start=True, stop=True).then_inc(setup, 1)

            def body(m, n, p):
                pm = 1 - p
                order = turn_order(m is not None, n is not None)

                def turn_is_free(use):
                    i = order.index(use)
                    if i == 0:
                        if m is not None:
                            pe.wait_ge(og_s, m * T + T)
                            pe.wait_ge(v_kept, m * 4 + 4)
                        else:
                            pe.wait_ge(setup, 14)
                        return
                    what, c = order[i - 1]
                    if what == "o":
                        pe.wait_ge(og_s, m * T + (c + 1 + T))
                    if what == "sum":
                        pe.wait_ge(rss, n * 4 + (c + 1))
                    if what == "k":
                        pe.wait_ge(k_kept, n * 2 + (c + 1))
                    if what == "v":
                        pe.wait_ge(v_kept, n * 4 + (c + 1))

                for s in range(SLOTS):
                    if m is not None:
                        t, k = divmod(s - CHAIN0, 3)
                        if 0 <= t < T:
                            if k == 0:
                                pe.wait_ge(st_s, m * T + (t + 1))
                                pe.wait_ge(o_s, m * T + (t + 2))
                                for c in range(2):
                                    last = pe.matmul(step[:, c], kq[:, pm, t, c], state[:, t % 2, :],
                                                     start=True, stop=True)
                                last.then_inc(ks_mm, 1)
                            if k == 1:
                                pe.wait_ge(r_s, m * T + (t + 1))
                                if t % 2 == 0:
                                    pe.wait_ge(lv_s, m * (LEVELS * T // 2) + (LEVELS * (t // 2 + 1) + 1))
                                pe.wait_ge(vn_s, m * T + (t + 1))
                                pe.matmul(new[:, :], zf[:, t], r[:, :], start=True, stop=True).then_inc(xr_mm, 1)
                            if k == 2:
                                pe.wait_ge(vn_s, m * T + (t + 1 + 1))
                                pe.wait_ge(o1_s, m * T + (t + 1 + 1))
                                pe.matmul(step[:, 1], kd[:, t], vn[:, :], start=True, stop=True)
                                pe.matmul(step[:, 0], attn[:, pm, t], vn[:, :], start=True, stop=True
                                          ).then_inc(osu_mm, 1)
                        t, k = divmod(s - CHAIN0 - 6, 3)
                        if 0 <= t < T and k == 0:
                            pe.wait_ge(on_s, m * T + (t + 1))
                            turn_is_free(("o", t))
                            for c in range(VT):
                                last = pe.transpose(turn[:, c * P:(c + 1) * P], o[:, t % 2, c * P:(c + 1) * P],
                                                    g.ident[:, :])
                            last.then_inc(o_mm, 1)
                    if n is not None:
                        q, third = divmod(s, 3)
                        j, half = divmod(q, 2)
                        if third == 0:
                            pe.wait_ge(w_low, n * UNITS + (j + 2))
                            pe.wait_ge(evac, n * HALVES + (q + 1))
                        last = three_passes(pe, proj[half][:, :], w_hi[slot_of(j)], w_lo[slot_of(j)],
                                            g.h_hi, g.h_lo, slice(half * HALF, (half + 1) * HALF), third)
                        if third == 2:
                            last.then_inc(proj_mm, 1)
                        if s in (8, 11, 14, 17):
                            q = (s - 8) // 3
                            pe.wait_ge(sq, n * 4 + (q + 1))
                            turn_is_free(("sum", q))
                            pe.matmul(turn[:, :], g.ones[:, :], sg[:, q % 2], start=True, stop=True).then_inc(nsum, 1)
                        if s in K_TURNS:
                            half = K_TURNS.index(s)
                            pe.wait_ge(kqn, n * 4 + (half + 1))
                            turn_is_free(("k", half))
                            for t in range(TH):
                                last = pe.transpose(turn[:, t * P:(t + 1) * P], kq[:, p, half * TH + t, 0],
                                                    g.ident[:, :])
                            last.then_inc(k_turned, 1)
                        if s in (20, 23, 26, 29):
                            c = (s - 20) // 3
                            pe.wait_ge(act_out, n * HALVES + (4 + c + 1 + 2))
                            turn_is_free(("v", c))
                            for t in range(TH):
                                last = pe.transpose(turn[:, t * P:(t + 1) * P], acc[:, c % 2, t * P:(t + 1) * P],
                                                    g.ident[:, :])
                            last.then_inc(v_turned, 1)
                        if s in DECAYS:
                            half = DECAYS.index(s)
                            if half:
                                pe.wait_ge(darg, n * T + TH)
                            else:
                                pe.wait_ge(hc_s, n * 5 + 5)
                                if not (isinstance(n, int) and n == 0):
                                    pe.wait_ge(ut, n * (T // 2))
                            for t in range(TH):
                                last = pe.matmul(gram[:, t * P:(t + 1) * P], spread(hc[:, p, C_LOG, half * TH + t], 1, P),
                                                 g.tri[:, :], start=True, stop=True)
                            last.then_inc(row_mm, 1)
                        b, k = divmod(s - GRAM0, 2)
                        if 0 <= b < T // 2 and k == 0:
                            pe.wait_ge(kqn, n * 4 + (3 + b // 2))
                            if b:
                                pe.wait_ge(ut, n * (T // 2) + b)
                            else:
                                pe.wait_ge(darg, n * T + T)
                            for e in range(2):
                                last = pe.matmul(gram[:, e * 2 * P:(e + 1) * 2 * P], kq[:, p, 2 * b + e, 0],
                                                 kq[:, p, 2 * b + e, :, :].rearrange("p c i -> p (c i)"),
                                                 start=True, stop=True)
                            last.then_inc(gram_mm, 1)
                    if m is not None:
                        b, k = divmod(s - LEVEL0, 6)
                        if 0 <= b < T // 2:
                            level, second = divmod(k, 2)
                            use = LEVELS * b + level
                            x = zx[:, 2 * b:2 * b + 2] if level == 0 else zx1[:, :, :, :]
                            if not second:
                                if level:
                                    pe.wait_ge(lv_s, m * (LEVELS * T // 2) + (use + 1))
                                else:
                                    if b < 2:
                                        pe.wait_ge(back[b], m * 32 + 32)
                                    pe.wait_ge(um_s, m * (T // 2) + (b + 1))
                                for e in range(2):
                                    last = pe.matmul(first[:, e, :], um[:, e, level], x[:, e, 1], start=True, stop=True)
                                last.then_inc(first_mm, 1)
                            else:
                                pe.wait_ge(first_c, m * (LEVELS * T // 2) + (use + 1))
                                if level == 0:
                                    pe.wait_ge(lv_s, m * (LEVELS * T // 2) + (use + 1))
                                for e in range(2):
                                    last = pe.matmul(lev[:, e, 0], bc[:, e], x[:, e, 0], start=True, stop=True)
                                    if level < LEVELS - 1:
                                        last = pe.matmul(lev[:, e, 1], x[:, e, 0], bc[:, e], start=True, stop=True)
                                last.then_inc(lv_mm, 1)

            heads(pe, body)

        @block.vector
        def _(dve):
            def split_low(idx, slot):
                dve.wait_ge(w_high, idx + 1)
                dve.tensor_tensor(w_lo[slot][:, :, :], raw[:, slot], w_hi[slot][:, :, :].bitcast(F32),
                                  ALU.subtract).then_inc(w_low, 1)

            dve.memset(x_raw[:, 0:CONV - 1], 0.0).then_inc(convs, 1)
            dve.memset(state[:, 0, :], 0.0).then_inc(st_s, 1)
            dve.memset(state[:, 1, :], 0.0).then_inc(setup, 1)
            for s_, c in ((act_out, 2), (o_s, 2), (og_s, T), (o1_s, 1), (vn_s, 1), (o_mm, 2),
                          (o_stored, 16),
                          (first_mm, 1), (osu_mm, 1), (lv_s, 1), (ostats, 6)):
                dve.sem_inc(s_, c)
            dve.wait_ge(setup, 2)
            logits = turn[:, 0:T * 2 * H].rearrange("p (t h) -> p t h", t=T)
            dve.tensor_scalar(tmp[:, 0], logits[:, :, 0:H], -1.0, ARG_MAX, ALU.mult, ALU.min)
            dve.tensor_tensor(tmp[:, 1], logits[:, :, H:2 * H], spread(g.head_bc[:, H:2 * H], 1, T),
                              ALU.add).then_inc(setup, 1)
            dve.wait_ge(setup, 10)
            dve.scalar_tensor_tensor(tmp[:, 2], tmp[:, 1], 0.0, tmp[:, 2], ALU.max, ALU.add).then_inc(setup, 1)
            dve.wait_ge(setup, 11)
            dve.scalar_tensor_tensor(cols[:, C_LOG], tmp[:, 2], -1.0, spread(neg_a[:, :], 1, T),
                                     ALU.mult, ALU.mult).then_inc(setup, 1)
            dve.wait_ge(setup, 13)
            cum = turn[:, 256:256 + T * H].rearrange("p (t h) -> p t h", t=T)
            total = turn[:, 384:384 + T * H].rearrange("p (t h) -> p t h", t=T)
            dve.tensor_copy(cols[:, C_CUM], cum)
            dve.tensor_copy(tmp[:, 0], total).then_inc(totals, 1)
            dve.wait_ge(totals, 1)
            dve.tensor_tensor(tmp[:, 1], tmp[:, 0], cols[:, C_CUM], ALU.subtract).then_inc(setup, 1)
            dve.wait_ge(setup, 17)
            dve.tensor_scalar(cols[:, C_NEXP], cols[:, C_EXP], -1.0, None, ALU.mult).then_inc(cols_s, 1)

            def body(m, n, p):
                pm = 1 - p
                for s in range(DELAYED):
                    if m is not None:
                        b, k = divmod(s - LEVEL0 - 2, 6)
                        if 0 <= b < T // 2 and k % 2 == 0:
                            level = k // 2
                            use = LEVELS * b + level
                            x = zx[:, 2 * b:2 * b + 2] if level == 0 else zx1[:, :, :, :]
                            dve.wait_ge(lv_mm, m * (LEVELS * T // 2) + (use + 1))
                            if level:
                                dve.wait_ge(lv_s, m * (LEVELS * T // 2) + (use + 1))
                            if level < LEVELS - 1:
                                dve.tensor_tensor(zx1[:, :, :, :], x, lev[:, :, :, :], ALU.subtract).then_inc(lv_s, 1)
                            else:
                                dve.tensor_tensor(zf[:, 2 * b:2 * b + 2, :], x[:, :, 0], lev[:, :, 0],
                                                  ALU.subtract).then_inc(lv_s, 1)
                        t, k = divmod(s - CHAIN0, 3)
                        if 0 <= t < T and k == 0:
                            dve.wait_ge(ks_mm, m * T + (t + 1))
                            dve.scalar_tensor_tensor(r[:, :], step[:, 0], hc[:, pm, C_NEXP, t:t + 1], v[:, pm, t, :],
                                                     ALU.mult, ALU.add).then_inc(r_s, 1)
                        if 0 <= t < T and k == 2:
                            dve.wait_ge(osu_mm, m * T + (t + 1 + 1))
                            dve.wait_ge(st_s, m * T + (t + 1))
                            if t == T - 1:
                                dve.memset(state[:, 0, :], 0.0).then_inc(st_s, 1)
                            else:
                                dve.scalar_tensor_tensor(state[:, (t + 1) % 2, :], state[:, t % 2, :],
                                                         hc[:, pm, C_LAST, t:t + 1], step[:, 1],
                                                         ALU.mult, ALU.add).then_inc(st_s, 1)
                            dve.wait_ge(o1_s, m * T + (t + 2))
                            dve.wait_ge(o_mm, m * T + (t - 1 + 2))
                            dve.tensor_tensor(o[:, t % 2, :], step[:, 0], o1[:, t % 2, :], ALU.add).then_inc(o_s, 1)
                        t, k = divmod(s - CHAIN0 - 6, 3)
                        if 0 <= t < T and k == 0:
                            dve.wait_ge(o_mm, m * T + (t + 1 + 2))
                            dve.wait_ge(o_stored, m * (16 * T) + 16 * (t + 1))
                            dve.tensor_tensor(og[:, :, :], turn[:, 0:DV].rearrange("p (c i) -> p c i", c=VT),
                                              z[:, pm, :, t * P:(t + 1) * P], ALU.mult).then_inc(og_s, 1)
                    if n is not None:
                        if s < SLOTS and s % 6 == 3:
                            j = s // 6 + 1
                            if j < UNITS or not (isinstance(n, int) and n == H - 1):
                                split_low(n * UNITS + (1 + j), slot_of(j % UNITS))
                        if s == 4:
                            dve.wait_ge(hc_s, n * 5 + 5)
                        q, k = divmod(s - 10, 3)
                        if 0 <= q < 4 and k == 0:
                            dve.wait_ge(rs, n * 4 + (q + 1))
                            dve.tensor_tensor(kq[:, p, (q % 2) * TH:(q % 2 + 1) * TH, q // 2, :],
                                              acc[:, q % 2].rearrange("p (t i) -> p t i", t=TH),
                                              sg[:, q % 2].rearrange("p (t i) -> p t i", t=TH),
                                              ALU.mult).then_inc(kqn, 1)
                        q, k = divmod(s - 4, 3)
                        if 0 <= q < HALVES and k == 0:
                            half, j = q % 2, q // 2
                            dve.wait_ge(act_out, n * HALVES + (q - 1 + 2))
                            if 2 <= q < 6:
                                dve.wait_ge(kqn, n * 4 + (q - 1))
                            dve.wait_ge(evac, n * HALVES + (q + 3))
                            if q in (6, 7):
                                dve.wait_ge(v_turned, n * 4 + (q - 5))
                            if q < 8:
                                for tap in range(CONV):
                                    if tap:
                                        dve.wait_ge(taps, n * 24 + (3 * q + tap))
                                    src = x_raw[:, half * HALF + tap:half * HALF + tap + HALF]
                                    w = hw[:, p, tap, j:j + 1]
                                    if tap == 0:
                                        ins = dve.tensor_scalar(acc[:, half], src, w, None, ALU.mult)
                                    else:
                                        ins = dve.scalar_tensor_tensor(acc[:, half], src, w, acc[:, half],
                                                                       ALU.mult, ALU.add)
                                    ins.then_inc(taps if tap < CONV - 1 else convs, 1)
                                dve.wait_ge(convs, n * 8 + (q + 2))
                            dve.tensor_scalar(sg[:, half], acc[:, half], -1.0, ARG_MAX, ALU.mult,
                                              ALU.min).then_inc(arg, 1)
                        q, k = divmod(s - 6, 3)
                        if 0 <= q < HALVES and k == 0:
                            half = q % 2
                            dve.wait_ge(sig, n * HALVES + (q + 1))
                            if q < 8:
                                dve.tensor_tensor(acc[:, half], acc[:, half], sg[:, half], ALU.mult).then_inc(act_out, 1)
                            else:
                                c = q // 2 - 4
                                dve.wait_ge(og_s, n * T)
                                dve.scalar_tensor_tensor(z[:, p, c, half * HALF:(half + 1) * HALF], acc[:, half],
                                                         g.gains[:, 16 + c:17 + c], sg[:, half],
                                                         ALU.mult, ALU.mult).then_inc(act_out, 1)
                        if s in K_TURNS:
                            half = K_TURNS.index(s)
                            tiles = slice(half * TH, (half + 1) * TH)
                            dve.wait_ge(k_turned, n * 2 + (half + 1))
                            if m is not None:
                                dve.wait_ge(osu_mm, m * T + ((half + 1) * TH + 1))
                            dve.tensor_tensor(kd[:, tiles, :], turn[:, :].rearrange("p (t c) -> p t c", t=TH),
                                              spread(hc[:, p, C_TAIL, tiles], 2, P), ALU.mult).then_inc(k_kept, 1)
                        b, k = divmod(s - GRAM0 - 1, 2)
                        if 0 <= b < T // 2 and k == 0:
                            dve.wait_ge(gram_mm, n * (T // 2) + (b + 1))
                            dve.wait_ge(dexp, n * 2 + (b // 2 + 1))
                            if not (isinstance(n, int) and n == 0):
                                dve.wait_ge(blocks_out, n * 16)
                            if m is not None:
                                dve.wait_ge(um_s, m * (T // 2) + (b + 1))
                            pair = gram[:, :].rearrange("p (e c i) -> p e c i", e=2, c=2)
                            for e in range(2):
                                t = 2 * b + e
                                dve.scalar_tensor_tensor(u[:, t], pair[:, e, 0], hc[:, p, C_BETA, t:t + 1], dec[:, t],
                                                         ALU.mult, ALU.mult)
                            dve.tensor_tensor(attn[:, p, 2 * b:2 * b + 2], pair[:, :, 1], dec[:, 2 * b:2 * b + 2],
                                              ALU.mult).then_inc(ut, 1)
                        if s in DECAYS:
                            half = DECAYS.index(s)
                            dve.wait_ge(row_mm, n * 2 + (half + 1))
                            for t in range(TH):
                                at = half * TH + t
                                dve.scalar_tensor_tensor(dec[:, at], gram[:, t * P:(t + 1) * P],
                                                         hc[:, p, C_CUM, at:at + 1], g.decay_mask[:, :],
                                                         ALU.subtract, ALU.add).then_inc(darg, 1)

            heads(dve, body)


def out_projection(nc, tag, o_turned, w, x_in, x_out, k_tiles, rope_tables=None):
    RING = 4
    GROUPS = k_tiles // RING
    with ExitStack() as ctx:
        m = Mem(nc, ctx, tag)
        w_raw = m.sb("w_raw", [P, RING, D])
        a_raw = m.sb("a_raw", [P, RING, HALF])
        w_hi = [m.sb(f"w_hi{i}", [P, D], F32R) for i in range(RING)]
        w_lo = [m.sb(f"w_lo{i}", [P, D], F32R) for i in range(RING)]
        a_hi = [m.sb(f"a_hi{i}", [P, HALF], F32R) for i in range(RING)]
        a_lo = [m.sb(f"a_lo{i}", [P, HALF], F32R) for i in range(RING)]
        x = m.sb("x", [P, 2, TH, D])
        y = [m.ps(f"y{i}", [P, HALF]) for i in range(2 * TH)]
        landed = [m.sem(f"landed{i}") for i in range(RING)]
        x_landed = [m.sem("x_landed0"), m.sem("x_landed1")]
        high, low = m.sem("high"), m.sem("low")
        used = m.sem("used")
        summed = m.sem("summed")
        stored = m.sem("stored")
        if rope_tables:
            rope_tables.scratch(m)
        block = ctx.enter_context(nc.Block())

        if rope_tables:
            @block.gpsimd
            def _(pool):
                rope_tables.angles(pool)

        def units(eng, unit, between=None):
            for half in range(2):
                unit(half, 0, True, False)
                if GROUPS > 2:
                    with eng.Fori(1, GROUPS - 1) as i:
                        unit(half, i, False, False)
                unit(half, GROUPS - 1, False, True)
                if between:
                    between(half)

        def index(half, i, c):
            return half * k_tiles + i * RING + c

        @block.sync
        def _(sp):
            def load(half, i, first, last):
                for c in range(RING):
                    if not (first and half == 0):
                        sp.wait_ge(low, index(half, i, c) + (1 - RING))
                    row = i * (RING * P) + c * P
                    sp.dma_start(w_raw[:, c, :], w[bass.ds(row, P), :]).then_inc(landed[c], 16)
                    sp.dma_start(a_raw[:, c, :], o_turned[bass.ds(row, P), half * HALF:(half + 1) * HALF]
                                 ).then_inc(landed[c], 16)
                if first:
                    sp.dma_start(x[:, half], x_in[half * HALF:(half + 1) * HALF, :]
                                 .rearrange("(t p) n -> p t n", p=P)).then_inc(x_landed[half], 16)

            if rope_tables:
                rope_tables.load(sp)
            units(sp, load)
            for half in range(2):
                for t in range(TH):
                    sp.wait_ge(summed, half * 2 * TH + 2 * t + 2)
                    row = half * HALF + t * P
                    sp.dma_start(x_out[row:row + P, :], x[:, half, t, :]).then_inc(stored, 16)
            sp.wait_ge(stored, 16 * T)

        @block.scalar
        def _(act):
            def split(half, i, first, last):
                for c in range(RING):
                    act.wait_ge(landed[c], i * 32 + (half * GROUPS * 32 + 32))
                    if not (first and half == 0):
                        act.wait_ge(used, index(half, i, c) + (1 - RING))
                    act.activation(a_hi[c][:, :], a_raw[:, c, :], ACT.Copy).then_inc(high, 1)
                    act.activation(w_hi[c][:, :], w_raw[:, c, :], ACT.Copy).then_inc(high, 1)
            units(act, split)
            if rope_tables:
                rope_tables.take(act)

        @block.vector
        def _(dve):
            def split(half, i, first, last):
                for c in range(RING):
                    dve.wait_ge(high, (i * RING + half * k_tiles + c) * 2 + 2)
                    dve.tensor_tensor(a_lo[c][:, :], a_raw[:, c, :], a_hi[c][:, :].bitcast(F32), ALU.subtract)
                    dve.tensor_tensor(w_lo[c][:, :], w_raw[:, c, :], w_hi[c][:, :].bitcast(F32),
                                      ALU.subtract).then_inc(low, 1)

            def add(half):
                dve.wait_ge(x_landed[half], 16)
                dve.wait_ge(used, (half + 1) * k_tiles)
                for b in range(2 * TH):
                    cell = x[:, half, b // 2, (b % 2) * HALF:(b % 2 + 1) * HALF]
                    dve.tensor_tensor(cell, y[b][:, :], cell, ALU.add).then_inc(summed, 1)
            units(dve, split, add)

        @block.tensor
        def _(pe):
            def multiply(half, i, first, last):
                for c in range(RING):
                    pe.wait_ge(low, index(half, i, c) + 1)
                    for b in range(2 * TH):
                        if first and half and c == 0:
                            pe.wait_ge(summed, b + 1)
                        ts = slice((b // 2) * P, (b // 2 + 1) * P)
                        ns = slice((b % 2) * HALF, (b % 2 + 1) * HALF)
                        for n, (a_, w_) in enumerate(((a_hi, w_hi), (a_hi, w_lo), (a_lo, w_hi))):
                            mm = pe.matmul(y[b][:, :], a_[c][:, ts], w_[c][:, ns],
                                           start=(first and c == 0 and n == 0),
                                           stop=(last and c == RING - 1 and n == 2))
                    mm.then_inc(used, 1)
            units(pe, multiply)


B_UNITS = 3 * NG + 1
B_HALVES = 2 * B_UNITS
B_SLOTS = 3 * B_HALVES
B_DELAYED = B_SLOTS + 6
SCORE = DK ** -0.5
PAIRS = 12
BATCHES = 9
BATCH0 = 25
NUMERATED = (BATCH0 + 12, BATCH0 + 22)
FINISH = (44, 48)


class RopeTables:

    def __init__(self, nc, ctx, g, positions):
        m = Mem(nc, ctx, "t")
        self.g, self.positions = g, positions
        self.cos, self.sin = m.sb("cos", [ROPE, S]), m.sb("sin", [ROPE, S])
        self.landed, self.step = m.sem("landed"), m.sem("step")

    def scratch(self, m):
        self.pos = m.sb("pos", [ROPE, S], I32)
        self.ang, self.turns, self.part = (m.sb(x, [ROPE, S]) for x in ("ang", "turns", "part"))
        self.rest = [m.sb("rest0", [ROPE, S]), m.sb("rest1", [ROPE, S])]

    def load(self, sp):
        sp.dma_start(self.pos[:, :], self.positions.partition_broadcast(ROPE)).then_inc(self.landed, 16)

    def angles(self, pool):
        TWO_PI = 2.0 * np.pi
        part1 = 6.28125
        part2 = float(np.float32(np.round((TWO_PI - part1) * 2.0 ** 20) / 2.0 ** 20))
        part3 = float(np.float32(TWO_PI - part1 - part2))
        ROUND = 1.5 * 2.0 ** 23
        PI = float(np.float32(3.1415925))
        ang, turns, part = self.ang[:, :], self.turns[:, :], self.part[:, :]
        steps = []

        def chained(ins):
            steps.append(ins)
            ins.then_inc(self.step, 1)
            pool.wait_ge(self.step, len(steps))

        pool.wait_ge(self.landed, 16)
        chained(pool.tensor_copy(ang, self.pos[:, :]))
        chained(pool.tensor_scalar(ang, ang, self.g.freq[:, 0:1], None, ALU.mult))
        for rest, shift in ((self.rest[0][:, :], 0.0), (self.rest[1][:, :], 0.25)):
            chained(pool.tensor_scalar(turns, ang, 1.0 / TWO_PI, shift, ALU.mult, ALU.add))
            chained(pool.tensor_scalar(turns, turns, ROUND, None, ALU.add))
            chained(pool.tensor_scalar(turns, turns, ROUND, None, ALU.subtract))
            left = ang
            for size in (part1, part2, part3):
                chained(pool.tensor_scalar(part, turns, size, None, ALU.mult))
                chained(pool.tensor_tensor(rest, left, part, ALU.subtract))
                left = rest
            chained(pool.tensor_scalar(rest, rest, shift * TWO_PI, PI, ALU.add, ALU.min))
            chained(pool.tensor_scalar(rest, rest, -PI, None, ALU.max))
            if shift == 0.0:
                chained(pool.tensor_scalar(rest, rest, self.g.freq[:, 1:2], None, ALU.mult))
        assert len(steps) == 2 + 2 * 11 + 1

    def take(self, act):
        act.wait_ge(self.step, 2 + 2 * 11 + 1)
        act.activation(self.sin[:, :], self.rest[0][:, :], ACT.Sin)
        act.activation(self.cos[:, :], self.rest[1][:, :], ACT.Sin)


def attention_heads(nc, r, rope_tables, weights, o_turned):
    with ExitStack() as ctx:
        m_ = Mem(nc, ctx, "b")
        raw, w_hi, w_lo = weights.raw, weights.hi, weights.lo
        qk = m_.sb("qk", [P, 2 * NG, S])
        v_raw = m_.sb("v_raw", [P, S])
        v = m_.sb("v", [P, NG, T, P])
        sc = m_.sb("sc", [P, 36 * P])
        kept = m_.sb("kept", [P, 2, 4, P])
        pairs_kept = m_.sb("pairs_kept", [P, T, P])
        acc = m_.sb("acc", [P, 2, HALF])
        sg = m_.sb("sg", [P, 2, HALF])
        sq_hi = m_.sb("sq_hi", [P, HALF], F32R)
        sq_lo = m_.sb("sq_lo", [P, HALF], F32R)
        swap = m_.sb("swap", [ROPE, HALF])
        z = m_.sb("z", [P, S])
        zl = m_.sb("zl", [P, S])
        fin = m_.sb("fin", [P, 2, HALF])
        den = m_.sb("den", [P, NG, T])
        den_by = m_.sb("den_by", [P, 2, T])
        ln_den = m_.sb("ln_den", [P, T])
        ln_row = m_.sb("ln_row", [P, S])
        mx = m_.sb("mx", [P, NG, T])
        mo = m_.sb("mo", [P, 2, T])
        nb = m_.sb("nb", [P, NG, T])
        mx_dram = nc.dram_tensor("maxima", [3, S], F32, kind="Internal").ap()
        den_dram = nc.dram_tensor("denominators", [3, S], F32, kind="Internal").ap()

        proj = [m_.ps(f"proj{i}", [P, HALF]) for i in range(2)]
        side = m_.ps("side", [P, HALF])
        ring = [m_.ps(f"ring{i}", [P, HALF]) for i in range(3)]
        num = [m_.ps(f"num{i}", [P, HALF]) for i in range(2)]

        sem = m_.sem
        w_landed, w_high, w_low = weights.landed, weights.high, weights.low
        proj_mm, evac = sem("proj_mm"), sem("evac")
        sq_high, sq_low = sem("sq_high"), sem("sq_low")
        nsum, rss, rs = sem("nsum"), sem("rss"), sem("rs")
        rope, ropes, qkn = sem("rope"), sem("ropes"), sem("qkn")
        v_turned, v_kept = sem("v_turned"), sem("v_kept")
        zarg, zexp, zln = sem("zarg"), sem("zexp"), sem("zln")
        score_mm, mxs = sem("score_mm"), sem("mxs")
        mx_out, mx_in, mmax = sem("mx_out"), sem("mx_in"), sem("mmax")
        nb_out, nb_in, nbs = sem("nb_out"), sem("nb_in"), sem("nbs")
        exps = sem("exps")
        p_turned, p_kept = sem("p_turned"), [sem("p_kept0"), sem("p_kept1")]
        pv = sem("pv")
        half_mm, lden, larg, lexp, nzr, ogs = (sem(x) for x in ("half_mm", "lden", "larg", "lexp", "nzr", "ogs"))
        den_out, den_in, den_sum = sem("den_out"), sem("den_in"), sem("den_sum")
        ln_out, ln_in = sem("ln_out"), sem("ln_in")
        o_stored = sem("o_stored")
        carrier = sem("carrier")
        block = ctx.enter_context(nc.Block())

        def col_of(n, j):
            if j < 2 * NG:
                return n * P + ((j % 2) * NG + j // 2) * D
            return n * P + j * D

        def slot_of(j):
            return j % 2

        def landed_of(n, j):
            return 16 * (n * (B_UNITS // 2) + j // 2 + 1)

        score_tiles = []
        at = 0
        for g, tile in [(0, i) for i in range(T)] + [(1, i) for i in range(T)] + [(2, i) for i in range(T)]:
            before = (g == 0 and tile > 0) or (g == 1 and tile >= TH)
            if g == 1:
                first = (tile % TH) * (2 * P) + (tile // TH) * P
            else:
                first = tile * P
            width = 2 * P if before else P
            score_tiles.append((g, tile, at, first, width, before))
            at += width
        assert at <= 36 * P
        tile_at = {(g, tile): (at, before) for g, tile, at, _, _, before in score_tiles}
        order = ([(0, i) for i in range(TH)] + [(1, i) for i in range(TH)] + [(2, i) for i in range(T)]
                 + [(0, i) for i in range(TH, T)] + [(1, i) for i in range(TH, T)])

        def out_cols(g, tile):
            if g == 0:
                return slice((tile % TH) * P, (tile % TH + 1) * P)
            return slice(tile % TH, HALF, TH) if g == 1 else slice(tile, HALF, T)

        def key_tile(g, tile, prev):
            return tile - (1 if g == 0 else TH) if prev else tile

        batches = [
            [(0, i, False) for i in range(0, TH)], [(0, i, True) for i in range(1, TH)],
            [(1, i, False) for i in range(0, TH)],
            [(2, i, False) for i in range(0, 4)], [(2, i, False) for i in range(4, T)],
            [(0, i, False) for i in range(TH, T)], [(0, i, True) for i in range(TH, T)],
            [(1, i, False) for i in range(TH, T)], [(1, i, True) for i in range(TH, T)],
        ]
        assert len(batches) == BATCHES

        def heads(eng, body):
            body(None, 0)
            with eng.Fori(0, H - 1) as i:
                body(i, i + 1)
            body(H - 1, None)

        def some(n):
            return not (isinstance(n, int) and n == 0)

        V_TURNS = tuple(3 * (13 + 2 * g) + 4 + c for g in range(NG) for c in range(2))

        def keep_batch(eng, m, i):
            eng.wait_ge(p_turned, m * BATCHES + (i + 1))
            eng.wait_ge(pv, m * (BATCHES + 1) + max(i - 1, 0) + 1)
            n = len(batches[i])
            if batches[i][0][0] == 2:
                out = pairs_kept[:, batches[i][0][1]:batches[i][0][1] + n, :]
            else:
                out = kept[:, i % 2, 0:n, :]
            src = ring[(PAIRS + i) % 3][:, 0:n * P].rearrange("p (t c) -> p t c", t=n)
            if eng.engine == nc.scalar.engine:
                eng.activation(out, src, ACT.Copy).then_inc(p_kept[i % 2], 1)
            else:
                eng.tensor_copy(out, src).then_inc(p_kept[i % 2], 1)

        def kept_count(m, i):
            return m * (BATCHES - BATCHES // 2 if i % 2 == 0 else BATCHES // 2) + i // 2 + 1

        @block.sync
        def _(sp):
            def load(n, j):
                sp.wait_ge(w_low, n * B_UNITS + (j - 1))
                sp.dma_start(raw[:, slot_of(j)], weights.w[:, bass.ds(col_of(n, j), P)]
                             .rearrange("(k p) c -> p k c", p=P)).then_inc(w_landed[slot_of(j)], 16)

            def body(m, n):
                last = isinstance(n, int) and n == H - 1
                for s in range(B_DELAYED):
                    if m is not None and s == 12:
                        sp.wait_ge(mxs, m * NG * T + NG * T)
                        sp.dma_start(mx_dram[0].rearrange("(t p) -> p t", p=P), mx[:, 0, :],
                                     allow_slow_non_contiguous=True).then_inc(mx_out, 16)
                        sp.dma_start(mx_dram[1].rearrange("(b p r) -> p b r", b=2, r=TH),
                                     mx[:, 1, :].rearrange("p (b r) -> p b r", b=2)).then_inc(mx_out, 16)
                        sp.wait_ge(mx_out, m * 32 + 32)
                        for c in range(2):
                            sp.dma_start(mo[:, c, :], mx_dram[c].rearrange("(p j) -> p j", j=T)).then_inc(mx_in, 16)
                    if m is not None and s == 17:
                        sp.wait_ge(nbs, m + 1)
                        sp.dma_start(mx_dram[2].rearrange("(p j) -> p j", j=T), nb[:, 2, :]).then_inc(nb_out, 16)
                        sp.wait_ge(nb_out, m * 16 + 16)
                        sp.dma_start(nb[:, 0, :], mx_dram[2].rearrange("(t p) -> p t", p=P),
                                     allow_slow_non_contiguous=True).then_inc(nb_in, 16)
                        sp.dma_start(nb[:, 1, :].rearrange("p (b r) -> p b r", b=2),
                                     mx_dram[2].rearrange("(b p r) -> p b r", b=2, r=TH)).then_inc(nb_in, 16)
                    if n is not None and s < B_SLOTS and s % 6 == 3:
                        j = s // 6 + 2
                        if j < B_UNITS:
                            load(n, j)
                        elif not last:
                            load(n + 1, j - B_UNITS)
                    if m is not None and s == 34:
                        sp.wait_ge(exps, m * (NG * T) + NG * T)
                        sp.dma_start(den_dram[0].rearrange("(t p) -> p t", p=P), den[:, 0, :],
                                     allow_slow_non_contiguous=True).then_inc(den_out, 16)
                        sp.dma_start(den_dram[1].rearrange("(b p r) -> p b r", b=2, r=TH),
                                     den[:, 1, :].rearrange("p (b r) -> p b r", b=2)).then_inc(den_out, 16)
                        sp.wait_ge(den_out, m * 32 + 32)
                        for c in range(2):
                            sp.dma_start(den_by[:, c, :], den_dram[c].rearrange("(p j) -> p j", j=T)
                                         ).then_inc(den_in, 16)
                    if m is not None and s == 38:
                        sp.wait_ge(lden, m + 1)
                        sp.dma_start(den_dram[2].rearrange("(p j) -> p j", j=T), ln_den[:, :]).then_inc(ln_out, 16)
                        sp.wait_ge(ln_out, m * 16 + 16)
                        sp.wait_ge(larg, m + 1)
                        sp.dma_start(ln_row[:, :], den_dram[2:3, :].partition_broadcast(P)).then_inc(ln_in, 16)
                    if m is not None and s in FINISH:
                        half = FINISH.index(s)
                        sp.wait_ge(ogs, m * 2 + (half + 1 + 2))
                        sp.dma_start(o_turned[bass.ds(m * P, P), half * HALF:(half + 1) * HALF], fin[:, half]
                                     ).then_inc(o_stored, 16)

            heads(sp, body)
            sp.wait_ge(o_stored, 16 * (1 + 2 * H))

        @block.scalar
        def _(act):
            def split_high(n, j, first=False):
                act.wait_ge(w_landed[slot_of(j)], landed_of(n, j))
                if not first:
                    act.wait_ge(proj_mm, n * B_HALVES + (2 * j - 2))
                act.activation(w_hi[slot_of(j)][:, :, :], raw[:, slot_of(j)], ACT.Copy).then_inc(w_high, 1)

            act.preload_act_table_set(EXP_LN)
            def body(m, n):
                last = isinstance(n, int) and n == H - 1
                for s in range(B_DELAYED):
                    if m is not None:
                        if 22 <= s < 34:
                            if s == 22:
                                act.wait_ge(nb_in, m * 32 + 32)
                                act.wait_ge(den_sum, m * 2 + 1)
                            for g, tile in order[2 * (s - 22):2 * (s - 22) + 2]:
                                at, before = tile_at[g, tile]
                                cell = sc[:, at:at + (2 * P if before else P)]
                                act.activation(cell, cell, ACT.Exp, scale=SCORE, bias=nb[:, g, tile:tile + 1],
                                               accum_out=den[:, g, tile:tile + 1]).then_inc(exps, 1)
                        i, k = divmod(s - BATCH0 - 1, 2)
                        if k == 0 and 0 <= i < BATCHES and i % 2 == 0:
                            keep_batch(act, m, i)
                        if s == 38:
                            act.wait_ge(den_sum, m * 2 + (2 + 1))
                            act.activation(ln_den[:, :], den_by[:, 0, :], ACT.Ln).then_inc(lden, 1)
                        if s == 43:
                            act.wait_ge(larg, m + (1 + 1))
                            act.activation(zl[:, :], zl[:, :], ACT.Exp, scale=-1.0).then_inc(lexp, 1)
                    if n is not None:
                        if s < B_SLOTS and s % 6 == 2:
                            j = s // 6 + 1
                            if j < B_UNITS:
                                split_high(n, j, not some(n) and j == 1)
                            elif not last:
                                split_high(n + 1, 0)
                        q, k = divmod(s - 3, 3)
                        if k == 0 and 0 <= q < B_HALVES:
                            half, j = q % 2, q // 2
                            act.wait_ge(proj_mm, n * B_HALVES + (q + 1))
                            if j < 2 * NG:
                                act.wait_ge(qkn, n * 12 + (q - 1 + 2))
                                gain = 18 + (j % 2) * NG + j // 2
                                act.activation(acc[:, half], proj[half][:, :], ACT.Copy,
                                               scale=r.gains[:, gain:gain + 1]).then_inc(rope, 1)
                                act.activation(sg[:, half], proj[half][:, :], ACT.Square).then_inc(evac, 1)
                                act.wait_ge(evac, n * B_HALVES + (q + 1))
                                act.wait_ge(nsum, n * 12 + (q + 1))
                                act.activation(sq_hi[:, :], sg[:, half], ACT.Copy).then_inc(sq_high, 1)
                            elif j < 3 * NG:
                                act.wait_ge(v_turned, n * 6 + (2 * (j - 2 * NG) + 2))
                                act.activation(v_raw[:, half * HALF:(half + 1) * HALF], proj[half][:, :],
                                               ACT.Copy).then_inc(evac, 1)
                            else:
                                act.wait_ge(ogs, n * 2 + 2)
                                act.activation(z[:, half * HALF:(half + 1) * HALF], proj[half][:, :],
                                               ACT.Copy).then_inc(evac, 1)
                        q, k = divmod(s - 6, 3)
                        if k == 0 and 0 <= q < 12:
                            act.wait_ge(nsum, n * 12 + (q + 1 + 1))
                            act.activation(sg[:, q % 2], side[:, :], ACT.Ln, scale=1.0 / DK, bias=EPS).then_inc(rss, 1)
                            act.wait_ge(rss, n * 12 + (q + 1))
                            act.activation(sg[:, q % 2], sg[:, q % 2], ACT.Exp, scale=-0.5).then_inc(rs, 1)
                        q, k = divmod(s - 5, 3)
                        if k == 0 and q >= B_HALVES - 2 and q < B_HALVES:
                            half = q % 2
                            cell = zl[:, half * HALF:(half + 1) * HALF]
                            act.wait_ge(zarg, n * 2 + (half + 1))
                            act.activation(cell, cell, ACT.Exp).then_inc(zexp, 1)
                            act.wait_ge(zexp, n * 2 + (half + 1))
                            act.activation(cell, cell, ACT.Ln, bias=1.0).then_inc(zln, 1)
                        if s in V_TURNS:
                            c = V_TURNS.index(s)
                            act.wait_ge(v_turned, n * 6 + (c + 1 + 2))
                            act.activation(v[:, c // 2, (c % 2) * TH:(c % 2 + 1) * TH, :],
                                           side[:, :].rearrange("p (t c) -> p t c", t=TH), ACT.Copy).then_inc(v_kept, 1)

            heads(act, body)

        @block.tensor
        def _(pe):
            def multiply_batch(m, i):
                half = 0 if i < 5 else 1
                if i in (0, 5):
                    pe.wait_ge(nzr, m * 2 + (half + 1))
                pe.wait_ge(p_kept[i % 2], kept_count(m, i) + 1)
                for c, (g, tile, prev) in enumerate(batches[i]):
                    if g == 2:
                        a, keys = pairs_kept[0:64, tile, 0:64], slice(0, 64)
                    else:
                        a, keys = kept[:, i % 2, c, :], slice(0, P)
                    cols = out_cols(g, tile)
                    start = i in (0, 5) and c == 0
                    stop = i == 4 and c == 3
                    mm = pe.matmul(num[half][:, cols], v[keys, g, key_tile(g, tile, prev), :], a, start=start,
                                   stop=stop, skip_group_check=True)
                mm.then_inc(pv, 1)
                if i == 4:
                    pe.wait_ge(pv, m * (BATCHES + 1) + (5 + 1))
                    pe.sem_inc(half_mm, 1)

            def multiply_pairs(m):
                for j in range(T):
                    mm = pe.matmul(num[1][:, out_cols(2, j)], v[:, 2, j, :], pairs_kept[:, j, 64:P], start=False,
                                   stop=(j == T - 1), skip_group_check=True)
                mm.then_inc(pv, 1)
                pe.wait_ge(pv, m * (BATCHES + 1) + (BATCHES + 1 + 1))
                pe.sem_inc(half_mm, 1)

            def body(m, n):
                for s in range(B_SLOTS):
                    if m is not None:
                        if s < PAIRS:
                            if s == 0:
                                pe.wait_ge(qkn, m * 12 + 12 + 2)
                            if s < 3:
                                pe.wait_ge(p_kept[0], m * 5 + 1)
                                pe.wait_ge(p_kept[1], m * 4 + 1)
                            else:
                                pe.wait_ge(mxs, m * (NG * T) + 2 * (s - 2))
                            for c in range(2):
                                g, tile, at, first, width, before = score_tiles[2 * s + c]
                                begin = first - P if before else first
                                mm = pe.matmul(ring[s % 3][:, c * 2 * P:c * 2 * P + width],
                                               qk[:, 2 * g, first:first + P],
                                               qk[:, 2 * g + 1, begin:begin + width], start=True, stop=True)
                            mm.then_inc(score_mm, 1)
                        i, k = divmod(s - BATCH0 - 2, 2)
                        if k == 0 and 0 <= i < BATCHES:
                            multiply_batch(m, i)
                        if s == BATCH0 + 2 * BATCHES + 1:
                            multiply_pairs(m)
                        i, k = divmod(s - BATCH0, 2)
                        if k == 0 and 0 <= i < BATCHES:
                            if i < 3:
                                pe.wait_ge(mxs, m * (NG * T) + NG * T)
                            else:
                                pe.wait_ge(p_kept[(i - 3) % 2], kept_count(m, i - 3) + 1)
                            done = max(order.index((g, tile)) for g, tile, _ in batches[i]) + 1
                            pe.wait_ge(exps, m * (NG * T) + done)
                            for c, (g, tile, prev) in enumerate(batches[i]):
                                at, before = tile_at[g, tile]
                                at += P if before and not prev else 0
                                mm = pe.transpose(ring[(PAIRS + i) % 3][:, c * P:(c + 1) * P], sc[:, at:at + P],
                                                  r.ident[:, :])
                            mm.then_inc(p_turned, 1)
                    if n is not None:
                        q, third = divmod(s, 3)
                        j, half = divmod(q, 2)
                        if third == 0:
                            pe.wait_ge(w_low, n * B_UNITS + (j + 1))
                            if q > 1 or some(n):
                                pe.wait_ge(evac, n * B_HALVES + (q - 1))
                        mm = three_passes(pe, proj[half][:, :], w_hi[slot_of(j)], w_lo[slot_of(j)],
                                          r.h_hi, r.h_lo, slice(half * HALF, (half + 1) * HALF), third)
                        if third == 2:
                            mm.then_inc(proj_mm, 1)
                        q, k = divmod(s - 5, 3)
                        if k == 0 and 0 <= q < 12:
                            pe.wait_ge(sq_low, n * 12 + (q + 1))
                            if q:
                                pe.wait_ge(rss, n * 12 + q)
                            elif some(n):
                                pe.wait_ge(v_kept, n * 6)
                            pe.matmul(side[:, :], r.ones_r[:, :], sq_hi[:, :], start=True, stop=False)
                            pe.matmul(side[:, :], r.ones_r[:, :], sq_lo[:, :], start=False, stop=True).then_inc(nsum, 1)
                        if s in V_TURNS:
                            c = V_TURNS.index(s)
                            g = c // 2
                            pe.wait_ge(evac, n * B_HALVES + (12 + 2 * g + 2))
                            if c:
                                pe.wait_ge(v_kept, n * 6 + c)
                            else:
                                pe.wait_ge(rss, n * 12 + 12)
                            for t in range(TH):
                                tile = (c % 2) * TH + t
                                if g == 0:
                                    tokens = slice(tile * P, (tile + 1) * P)
                                elif g == 1:
                                    b, res = divmod(tile, TH)
                                    tokens = slice(b * HALF + res, (b + 1) * HALF, TH)
                                else:
                                    tokens = slice(tile, S, T)
                                mm = pe.transpose(side[:, t * P:(t + 1) * P], v_raw[:, tokens], r.ident[:, :])
                            mm.then_inc(v_turned, 1)

            heads(pe, body)

        @block.vector
        def _(dve):
            for s_, c in ((nsum, 1), (qkn, 2), (v_turned, 2), (ogs, 2), (pv, 1), (nzr, 2), (larg, 1), (den_sum, 1), (p_kept[0], 1),
                          (p_kept[1], 1), (o_stored, 16)):
                dve.sem_inc(s_, c)

            def split_low(n, j):
                dve.wait_ge(w_high, n * B_UNITS + (j + 1))
                dve.tensor_tensor(w_lo[slot_of(j)][:, :, :], raw[:, slot_of(j)], w_hi[slot_of(j)][:, :, :].bitcast(F32),
                                  ALU.subtract).then_inc(w_low, 1)

            def body(m, n):
                last = isinstance(n, int) and n == H - 1
                for s in range(B_DELAYED):
                    if m is not None:
                        if s < PAIRS:
                            if s == 0:
                                dve.wait_ge(pv, m * (BATCHES + 1) + 1)
                                if some(m):
                                    dve.wait_ge(mmax, m * 2)
                            dve.wait_ge(score_mm, m * PAIRS + (s + 1))
                            dve.sem_inc(carrier, 1)
                            for c in range(2):
                                g, tile, at, first, width, before = score_tiles[2 * s + c]
                                mask = r.pair_mask[:, :] if g == 2 else r.band_mask[:, 2 * P - width:2 * P]
                                dve.tensor_tensor_reduce(sc[:, at:at + width], ring[s % 3][:, c * 2 * P:c * 2 * P + width],
                                                         mask, 1.0, -BIG, ALU.add, ALU.max,
                                                         mx[:, g, tile:tile + 1]).then_inc(mxs, 1)
                        if s == 17:
                            dve.wait_ge(mx_in, m * 32 + 32)
                            dve.wait_ge(mxs, m * (NG * T) + NG * T)
                            dve.tensor_tensor(mo[:, 0, :], mo[:, 0, :], mo[:, 1, :], ALU.max).then_inc(mmax, 1)
                            dve.wait_ge(mmax, m * 2 + 1)
                            dve.tensor_tensor(mo[:, 0, :], mo[:, 0, :], mx[:, 2, :], ALU.max).then_inc(mmax, 1)
                            dve.wait_ge(mmax, m * 2 + 2)
                            if some(m):
                                dve.wait_ge(exps, m * (NG * T))
                            dve.tensor_scalar(nb[:, 2, :], mo[:, 0, :], -SCORE, None, ALU.mult).then_inc(nbs, 1)
                        i, k = divmod(s - BATCH0 - 1, 2)
                        if k == 0 and 0 <= i < BATCHES and i % 2:
                            keep_batch(dve, m, i)
                        if s == 37:
                            dve.wait_ge(den_in, m * 32 + 32)
                            dve.tensor_tensor(den_by[:, 0, :], den_by[:, 0, :], den_by[:, 1, :], ALU.add).then_inc(den_sum, 1)
                            dve.wait_ge(den_sum, m * 2 + (1 + 1))
                            dve.tensor_tensor(den_by[:, 0, :], den_by[:, 0, :], den[:, 2, :], ALU.add).then_inc(den_sum, 1)
                        if s == 42:
                            dve.wait_ge(ln_in, m * 16 + 16)
                            dve.wait_ge(zln, m * 2 + 2)
                            dve.tensor_tensor(zl[:, :], zl[:, :], ln_row[:, :], ALU.add).then_inc(larg, 1)
                        if s in NUMERATED:
                            half = NUMERATED.index(s)
                            dve.wait_ge(half_mm, m * 2 + (half + 1))
                            dve.wait_ge(o_stored, m * 32 + 16)
                            dve.tensor_tensor(fin[:, half], num[half][:, :], z[:, half * HALF:(half + 1) * HALF],
                                              ALU.mult).then_inc(nzr, 1)
                        if s in FINISH:
                            half = FINISH.index(s)
                            dve.wait_ge(lexp, m + 1)
                            dve.wait_ge(nzr, m * 2 + (half + 1 + 2))
                            dve.tensor_tensor(fin[:, half], fin[:, half], zl[:, half * HALF:(half + 1) * HALF],
                                              ALU.mult).then_inc(ogs, 1)
                    if n is not None:
                        if s < B_SLOTS and s % 6 == 3:
                            j = s // 6 + 1
                            if j < B_UNITS:
                                split_low(n, j)
                            elif not last:
                                split_low(n + 1, 0)
                        q, k = divmod(s - 4, 3)
                        if k == 0 and 0 <= q < 12:
                            dve.wait_ge(sq_high, n * 12 + (q + 1))
                            dve.tensor_tensor(sq_lo[:, :], sg[:, q % 2], sq_hi[:, :].bitcast(F32),
                                              ALU.subtract).then_inc(sq_low, 1)
                            half = q % 2
                            cols = slice(half * HALF, (half + 1) * HALF)
                            dve.wait_ge(rope, n * 12 + (q + 1))
                            if q:
                                dve.wait_ge(ropes, n * 48 + 4 * q)
                            elif some(n):
                                dve.wait_ge(ropes, n * 48)
                            dve.sem_inc(carrier, 1)
                            x = acc[0:ROPE, half]
                            dve.stream_shuffle(swap[:, :], x, [(i + HR) % ROPE for i in range(ROPE)]).then_inc(ropes, 1)
                            dve.wait_ge(ropes, n * 48 + (4 * q + 1))
                            dve.tensor_tensor(swap[:, :], swap[:, :], rope_tables.sin[:, cols], ALU.mult).then_inc(ropes, 1)
                            dve.tensor_tensor(x, x, rope_tables.cos[:, cols], ALU.mult).then_inc(ropes, 1)
                            dve.wait_ge(ropes, n * 48 + (4 * q + 3))
                            dve.tensor_tensor(x, x, swap[:, :], ALU.add).then_inc(ropes, 1)
                        q, k = divmod(s - 7, 3)
                        if k == 0 and 0 <= q < 12:
                            half, j = q % 2, q // 2
                            g = j // 2
                            dve.wait_ge(rs, n * 12 + (q + 1))
                            dve.wait_ge(ropes, n * 48 + (4 * q + 4))
                            if m is not None:
                                dve.wait_ge(score_mm, m * PAIRS + 4 * (g + 1))
                            a, b_ = acc[:, half], sg[:, half]
                            if g == 0:
                                out = qk[:, j, half * HALF:(half + 1) * HALF]
                            elif g == 1:
                                out = qk[:, j, :].rearrange("p (r i) -> p i r", r=TH)[:, half * P:(half + 1) * P, :]
                                a, b_ = (t.rearrange("p (i r) -> p i r", r=TH) for t in (a, b_))
                            else:
                                out = qk[:, j, :].rearrange("p (r i) -> p i r", r=T)[:, half * 64:(half + 1) * 64, :]
                                a, b_ = (t.rearrange("p (i r) -> p i r", r=T) for t in (a, b_))
                            dve.tensor_tensor(out, a, b_, ALU.mult).then_inc(qkn, 1)
                        q, k = divmod(s - 4, 3)
                        if k == 0 and B_HALVES - 2 <= q < B_HALVES:
                            half = q % 2
                            cols = slice(half * HALF, (half + 1) * HALF)
                            dve.wait_ge(evac, n * B_HALVES + (q + 1))
                            if m is not None:
                                dve.wait_ge(ogs, m * 2 + (2 + 2))
                            dve.tensor_scalar(zl[:, cols], z[:, cols], -1.0, ARG_MAX, ALU.mult,
                                              ALU.min).then_inc(zarg, 1)

            heads(dve, body)


def allocate(nc, ctx):
    m = Mem(nc, ctx, "g")
    g = type("Resident", (), {})()
    g.h_hi = m.sb("h_hi", [P, KD, S], F32R)
    g.h_lo = m.sb("h_lo", [P, KD, S], F32R)
    g.ones = m.sb("ones", [P, P])
    g.ones_r = m.sb("ones_r", [P, P], F32R)
    g.ident = m.sb("ident", [P, P])
    g.tri = m.sb("tri", [P, P])
    g.decay_mask = m.sb("decay_mask", [P, P])
    g.level_mask = m.sb("level_mask", [P, LEVELS, P])
    g.gains = m.sb("gains", [P, 24])
    g.conv = m.sb("conv", [P, CONV, CT])
    g.head_bc = m.sb("head_bc", [P, 2 * H])
    g.freq = m.sb("freq", [ROPE, 2])
    g.band_mask = m.sb("band_mask", [P, 2 * P])
    g.pair_mask = m.sb("pair_mask", [P, P])
    return g


def program(nc, x, positions, norm_g, a_w_in, a_conv_w, a_log, a_dt_bias, a_norm_g, a_w_out,
            b_w_in, b_q_norm_g, b_k_norm_g, b_w_out, out):
    a_out = nc.dram_tensor("a_out", [A_VW, S], F32, kind="Internal").ap()
    x1 = nc.dram_tensor("x1", [S, D], F32, kind="Internal").ap()
    b_out = nc.dram_tensor("b_out", [D, S], F32, kind="Internal").ap()
    with ExitStack() as ctx:
        g = allocate(nc, ctx)
        constants(nc, g, norm_g, a_norm_g, b_q_norm_g, b_k_norm_g, a_conv_w, a_log, a_dt_bias)
        with ExitStack() as layer:
            first = ((2 * A_QK + 2 * A_VW, 2 * H), (A_QK, P))
            weights = WeightSlots(nc, layer, "wa", a_w_in[0], first, True)
            norm_and_turn(nc, "n0", g, x[0], 0, weights)
            delta_heads(nc, g, weights, a_out)
        rope_tables = RopeTables(nc, ctx, g, positions)
        out_projection(nc, "p0", a_out, a_w_out[0], x[0], x1, A_VW // P, rope_tables)
        with ExitStack() as layer:
            weights = WeightSlots(nc, layer, "wb", b_w_in[0], ((0, P), (NG * D, P)), False)
            norm_and_turn(nc, "n1", g, x1, 1, weights)
            attention_heads(nc, g, rope_tables, weights, b_out)
        out_projection(nc, "p1", b_out, b_w_out[0], x1, out[0], D // P)


_INS = ["x", "positions", "norm_g", "a_w_in", "a_conv_w", "a_log", "a_dt_bias", "a_norm_g", "a_w_out",
        "b_w_in", "b_q_norm_g", "b_k_norm_g", "b_w_out"]


def kernel(**inputs):
    import numpy as _np
    import concourse.bacc as _bacc
    from concourse import mybir as _mybir
    from concourse.bass_utils import run_bass_kernel_spmd as _run

    nc = _bacc.Bacc("TRN2", target_bir_lowering=False, num_devices=1)
    arrays, args = {}, []
    for name in _INS:
        a = _np.ascontiguousarray(inputs[name])
        arrays[f"in_{name}_dram"] = a
        args.append(nc.dram_tensor(f"in_{name}_dram", a.shape, _mybir.dt.from_np(a.dtype), kind="ExternalInput").ap())
    out = nc.dram_tensor("out_0_dram", (1, S, D), _mybir.dt.float32, kind="ExternalOutput").ap()
    program(nc, *args, out)
    r = _run(nc, [arrays], core_ids=[0])
    return r.results[0]["out_0_dram"]
```
